# Optimizing a Trainium2 kernel written in Bass

```python
import math
import jax, jax.numpy as jnp
from jax import lax
import numpy as np

D_MODEL = 2048
BATCH = 1
SEQ = 256
DEPTH = 1

HEAD_DIM = 64
MOBA_HEADS = 16
MOBA_BLOCK = 256
MOBA_TOPK = 3
MOBA_Q_CHUNK = 128
SWA_Q_HEADS = 16
SWA_KV_HEADS = 4
SWA_WINDOW = 128
SWA_BLOCK = 128
N_GROUPS = 4
EXPERTS_PER_GROUP = 8
N_EXPERTS = N_GROUPS * EXPERTS_PER_GROUP
EXPERT_TOP_K = 2
D_EXPERT = D_MODEL // 4
MOE_BLOCK = 128
RMS_EPS = 1e-6

MOBA_W = MOBA_HEADS * HEAD_DIM
SWA_Q_W = SWA_Q_HEADS * HEAD_DIM
SWA_KV_W = SWA_KV_HEADS * HEAD_DIM
IN_SIZES = [MOBA_W, MOBA_W, MOBA_W, SWA_Q_W, SWA_KV_W, SWA_KV_W, D_MODEL, D_MODEL]
IN_COLS = sum(IN_SIZES)

kernel_name = "hybrid_moba_swa_sink_hiermoe_block"

def rmsnorm(x, g):
    x32 = x.astype(jnp.float32)
    y = x32 * lax.rsqrt(jnp.mean(x32 * x32, axis=-1, keepdims=True) + RMS_EPS)
    return y.astype(x.dtype) * g

def alibi_slopes(n):
    return jnp.exp2(-8.0 * jnp.arange(1, n + 1, dtype=jnp.float32) / n)

def moba_attention(q, k, v, slopes):
    B, S, H, Dh = q.shape
    BS, QC = MOBA_BLOCK, MOBA_Q_CHUNK
    s_pad = -(-S // BS) * BS
    q, k, v = (jnp.swapaxes(t, 1, 2) for t in (q, k, v))
    if s_pad != S:
        pad = ((0, 0), (0, 0), (0, s_pad - S), (0, 0))
        q, k, v = (jnp.pad(t, pad) for t in (q, k, v))
    nb = s_pad // BS
    n_top = min(MOBA_TOPK, nb)
    scale = Dh ** -0.5
    kb = k.reshape(B, H, nb, BS, Dh)
    vb = v.reshape(B, H, nb, BS, Dh)
    k_mean = jnp.mean(kb.astype(jnp.float32), axis=3)
    gate = jnp.einsum('bhsd,bhnd->bhsn', q.astype(jnp.float32), k_mean)
    q_blk = jnp.arange(s_pad) // BS
    past = jnp.arange(nb)[None, :] < q_blk[:, None]
    gate = jnp.where(past, gate, -jnp.inf)
    _, sel = lax.top_k(gate, n_top)
    valid = sel < q_blk[:, None]
    nc = s_pad // QC
    to_chunks = lambda t: jnp.moveaxis(t.reshape(B, H, nc, QC, *t.shape[3:]), 2, 0)
    q_c, sel_c, valid_c = to_chunks(q), to_chunks(sel), to_chunks(valid)
    bi = jnp.arange(B)[:, None, None, None]
    hi = jnp.arange(H)[None, :, None, None]
    sl5 = slopes[None, :, None, None, None]
    sl4 = slopes[None, :, None, None]

    def chunk_fn(args):
        ci, qc, selc, validc = args
        t = ci * QC + jnp.arange(QC)
        blk = (ci * QC) // BS
        k_sel = kb[bi, hi, selc]
        v_sel = vb[bi, hi, selc]
        s_past = jnp.einsum('bhqd,bhqjkd->bhqjk', qc, k_sel).astype(jnp.float32) * scale
        key_pos = selc[..., None] * BS + jnp.arange(BS)
        dist = (t[:, None, None] - key_pos).astype(jnp.float32)
        s_past = jnp.where(validc[..., None], s_past - sl5 * dist, -jnp.inf)
        s_past = s_past.reshape(B, H, QC, n_top * BS)
        k_own = lax.dynamic_index_in_dim(kb, blk, axis=2, keepdims=False)
        v_own = lax.dynamic_index_in_dim(vb, blk, axis=2, keepdims=False)
        s_own = jnp.einsum('bhqd,bhkd->bhqk', qc, k_own).astype(jnp.float32) * scale
        d_own = (t[:, None] - (blk * BS + jnp.arange(BS))[None, :]).astype(jnp.float32)
        s_own = jnp.where(d_own >= 0, s_own - sl4 * d_own, -jnp.inf)
        p = jax.nn.softmax(jnp.concatenate([s_past, s_own], axis=-1), axis=-1)
        p_past = p[..., :n_top * BS].reshape(B, H, QC, n_top, BS).astype(v.dtype)
        p_own = p[..., n_top * BS:].astype(v.dtype)
        return (jnp.einsum('bhqjk,bhqjkd->bhqd', p_past, v_sel)
                + jnp.einsum('bhqk,bhkd->bhqd', p_own, v_own))

    o = lax.map(chunk_fn, (jnp.arange(nc), q_c, sel_c, valid_c))
    o = jnp.moveaxis(o, 0, 2).reshape(B, H, s_pad, Dh)[:, :, :S]
    return jnp.swapaxes(o, 1, 2).reshape(B, S, H * Dh)

def swa_sink_attention(q, k, v, sinks, slopes):
    B, S, Hq, Dh = q.shape
    Hkv = k.shape[2]
    G = Hq // Hkv
    W = SWA_BLOCK
    nb = S // W
    scale = Dh ** -0.5
    qb = q.reshape(B, nb, W, Hkv, G, Dh)
    kb = k.reshape(B, nb, W, Hkv, Dh)
    vb = v.reshape(B, nb, W, Hkv, Dh)
    shift = lambda t: jnp.pad(t[:, :-1], ((0, 0), (1, 0), (0, 0), (0, 0), (0, 0)))
    kk = jnp.concatenate([shift(kb), kb], axis=2)
    vv = jnp.concatenate([shift(vb), vb], axis=2)
    s = jnp.einsum('bnqhgd,bnkhd->bhgnqk', qb, kk).astype(jnp.float32) * scale
    dist = (jnp.arange(W)[:, None] + W - jnp.arange(2 * W)[None, :])
    in_win = (dist >= 0) & (dist < SWA_WINDOW)
    blk_ok = (jnp.arange(nb)[:, None, None] > 0) | (jnp.arange(2 * W)[None, None, :] >= W)
    mask = in_win[None] & blk_ok
    sl = slopes.reshape(Hkv, G)[:, :, None, None, None]
    s = jnp.where(mask, s - sl * dist.astype(jnp.float32), -jnp.inf)
    sink = jnp.broadcast_to(sinks.reshape(Hkv, G, 1, 1, 1).astype(jnp.float32), s.shape[:-1] + (1,))
    p = jax.nn.softmax(jnp.concatenate([s, sink], axis=-1), axis=-1)[..., :-1]
    o = jnp.einsum('bhgnqk,bnkhd->bnqhgd', p.astype(v.dtype), vv)
    return o.reshape(B, S, Hq * Dh)

def token_mixer(h, w_in, sinks, w_o_moba, w_o_swa, w_out, slopes_moba, slopes_swa):
    B, S, _ = h.shape
    offs = [int(o) for o in np.cumsum(IN_SIZES)[:-1]]
    qA, kA, vA, qB, kB, vB, gA, gB = jnp.split(h @ w_in, offs, axis=-1)
    heads = lambda t, n: t.reshape(B, S, n, HEAD_DIM)
    oA = moba_attention(heads(qA, MOBA_HEADS), heads(kA, MOBA_HEADS), heads(vA, MOBA_HEADS), slopes_moba)
    oB = swa_sink_attention(heads(qB, SWA_Q_HEADS), heads(kB, SWA_KV_HEADS), heads(vB, SWA_KV_HEADS),
                            sinks, slopes_swa)
    y = jax.nn.sigmoid(gA) * (oA @ w_o_moba) + jax.nn.sigmoid(gB) * (oB @ w_o_swa)
    return y @ w_out

def hier_moe(h, w_rg, b_rg, w_re, b_re, w_gate, w_up, w_down):
    B, S, D = h.shape
    T = B * S
    E, K, BLK = EXPERTS_PER_GROUP, EXPERT_TOP_K, MOE_BLOCK
    xt = h.reshape(T, D)
    g_logits = (xt @ w_rg).astype(jnp.float32) + b_rg
    g_sel = jnp.argmax(g_logits, axis=-1)
    g_w = jnp.take_along_axis(jax.nn.softmax(g_logits, axis=-1), g_sel[:, None], axis=-1)
    e_logits = ((xt @ w_re).astype(jnp.float32) + b_re).reshape(T, N_GROUPS, E)
    e_logits = jnp.take_along_axis(e_logits, g_sel[:, None, None], axis=1)[:, 0]
    e_top, e_idx = lax.top_k(e_logits, K)
    e_w = jax.nn.softmax(e_top, axis=-1) * g_w
    eid = (g_sel[:, None] * E + e_idx).reshape(-1)
    tok = jnp.repeat(jnp.arange(T), K)
    wts = e_w.reshape(-1)
    A = T * K
    order = jnp.argsort(eid)
    eid_s, tok_s, w_s = eid[order], tok[order], wts[order]
    counts = jnp.zeros((N_EXPERTS,), jnp.int32).at[eid].add(1)
    start = jnp.cumsum(counts) - counts
    padded = ((counts + BLK - 1) // BLK) * BLK
    pend = jnp.cumsum(padded)
    pstart = pend - padded
    dest = pstart[eid_s] + (jnp.arange(A) - start[eid_s])
    n_blocks = -(-A // BLK) + N_EXPERTS
    P = n_blocks * BLK
    buf_tok = jnp.zeros((P,), jnp.int32).at[dest].set(tok_s.astype(jnp.int32))
    buf_w = jnp.zeros((P,), h.dtype).at[dest].set(w_s.astype(h.dtype))
    block_expert = jnp.minimum(jnp.searchsorted(pend, jnp.arange(n_blocks) * BLK, side='right'),
                               N_EXPERTS - 1)
    xb = xt[buf_tok].reshape(n_blocks, BLK, D)

    def expert_block(args):
        xblk, e = args
        return (jax.nn.silu(xblk @ w_gate[e]) * (xblk @ w_up[e])) @ w_down[e]

    yb = lax.map(expert_block, (xb, block_expert)).reshape(P, D) * buf_w[:, None]
    return jax.ops.segment_sum(yb, buf_tok, num_segments=T).reshape(B, S, D)

def setup_inputs(seed: int = 0) -> dict:
    key = jax.random.key(seed)
    ks = jax.random.split(key, 20)
    L, D = DEPTH, D_MODEL
    f32 = jnp.float32
    nrm = lambda k, shape, fan_in: jax.random.normal(k, shape, f32) * fan_in ** -0.5
    gain = lambda k: 1.0 + 0.05 * jax.random.normal(k, (L, D), f32)
    return {
        "x": jax.random.normal(ks[0], (BATCH, SEQ, D), f32),
        "c": jax.random.normal(ks[1], (BATCH, D), f32),
        "w_ada": 0.5 * nrm(ks[2], (L, D, 6 * D), D),
        "b_ada": 0.02 * jax.random.normal(ks[3], (L, 6 * D), f32),
        "g_pre_mix": gain(ks[4]),
        "g_post_mix": gain(ks[5]),
        "w_in": nrm(ks[6], (L, D, IN_COLS), D),
        "swa_sinks": 0.5 * jax.random.normal(ks[7], (L, SWA_Q_HEADS), f32),
        "w_o_moba": nrm(ks[8], (L, MOBA_W, D), MOBA_W),
        "w_o_swa": nrm(ks[9], (L, SWA_Q_W, D), SWA_Q_W),
        "w_out": nrm(ks[10], (L, D, D), D),
        "g_pre_ffn": gain(ks[11]),
        "g_post_ffn": gain(ks[12]),
        "w_router_group": nrm(ks[13], (L, D, N_GROUPS), D),
        "b_router_group": 0.01 * jax.random.normal(ks[14], (L, N_GROUPS), f32),
        "w_router_expert": nrm(ks[15], (L, D, N_EXPERTS), D),
        "b_router_expert": 0.01 * jax.random.normal(ks[16], (L, N_EXPERTS), f32),
        "w_gate": nrm(ks[17], (L, N_EXPERTS, D, D_EXPERT), D),
        "w_up": nrm(ks[18], (L, N_EXPERTS, D, D_EXPERT), D),
        "w_down": nrm(ks[19], (L, N_EXPERTS, D_EXPERT, D), D_EXPERT),
    }

def reference(x, c, w_ada, b_ada, g_pre_mix, g_post_mix, w_in, swa_sinks, w_o_moba, w_o_swa, w_out,
              g_pre_ffn, g_post_ffn, w_router_group, b_router_group, w_router_expert, b_router_expert,
              w_gate, w_up, w_down):
    slopes_moba = alibi_slopes(MOBA_HEADS)
    slopes_swa = alibi_slopes(SWA_Q_HEADS)
    cond = jax.nn.silu(c)
    for l in range(DEPTH):
        mod = cond @ w_ada[l] + b_ada[l]
        sh_m, sc_m, gt_m, sh_f, sc_f, gt_f = (m[:, None, :] for m in jnp.split(mod, 6, axis=-1))
        h = rmsnorm(x, g_pre_mix[l]) * (1.0 + sc_m) + sh_m
        y = token_mixer(h, w_in[l], swa_sinks[l], w_o_moba[l], w_o_swa[l], w_out[l], slopes_moba, slopes_swa)
        x = x + gt_m * rmsnorm(y, g_post_mix[l])
        h = rmsnorm(x, g_pre_ffn[l]) * (1.0 + sc_f) + sh_f
        y = hier_moe(h, w_router_group[l], b_router_group[l], w_router_expert[l], b_router_expert[l],
                     w_gate[l], w_up[l], w_down[l])
        x = x + gt_f * rmsnorm(y, g_post_ffn[l])
    return x


_drawn_inputs = setup_inputs


def setup_inputs(seed=0):
    import zlib

    import numpy as np

    out = dict(_drawn_inputs(seed))
    spreads = {}
    factors = {'g_post_ffn': 4.168}
    for name, (base, spread) in spreads.items():
        noise = np.random.default_rng([zlib.crc32(name.encode()), seed]).standard_normal(out[name].shape)
        drawn = base * np.exp(spread * noise) if base else spread * noise
        out[name] = __import__('jax').numpy.asarray(drawn.astype(out[name].dtype))
    for name, factor in factors.items():
        out[name] = (out[name] * factor).astype(out[name].dtype)
    return out
```

```python
import concourse.bass as bass
from concourse import mybir

F32 = mybir.dt.float32
F32R = mybir.dt.float32r
I32 = mybir.dt.int32
ALU = mybir.AluOpType
ACT = mybir.ActivationFunctionType
AX = mybir.AxisListType

P = 128
D = 2048
T = 256
TT = T // P
KB = D // P
NB = 512
DB = D // NB
IN_COLS = 8704
HD = 64
HEADS = 16
PAIRS = HEADS // 2
KV = 4
GROUPS, PER_GROUP = 4, 8
E = GROUPS * PER_GROUP
FE = 512
CAP = 64
EPS = 1e-6
MASKED = 1e30
ADA_BLOCKS = 6 * D // NB
QUARTERS = 4
ADA_FIRST = 2 * QUARTERS
SPLITS = 4
SLOT = 8 * NB
MAX_OVER = TT * P * 2 // (CAP + 1) + 1

COL_QA, COL_KA, COL_VA, COL_QB, COL_KVB, COL_G = 0, 1024, 2048, 3072, 4096, 4608


def decoder_block(nc, x, c, w_ada, b_ada, g_pre_mix, g_post_mix, w_in, swa_sinks, w_o_moba, w_o_swa, w_out,
                  g_pre_ffn, g_post_ffn, w_router_group, b_router_group, w_router_expert, b_router_expert,
                  w_gate, w_up, w_down, out):
    base = 16512

    def place(name, shape, dtype, at):
        return nc.alloc_sbuf_tensor_at(name, shape, dtype, offset=base + at)

    RING, V, XRES, SM = 0, 131072, 186368, 202752
    ring = place("ring", [P, 8, SLOT], F32, RING)
    xres = place("xres", [P, TT, D], F32, XRES)
    U0 = 65536
    hT_hi = place("hT_hi", [P, KB, T], F32R, U0)
    hT_lo = place("hT_lo", [P, KB, T], F32R, U0 + 16384)
    w_hi = place("w_hi", [P, SPLITS, NB], F32R, U0 + 32768)
    w_lo = place("w_lo", [P, SPLITS, NB], F32R, U0 + 40960)
    gates = place("gates", [P, TT, 2 * D], F32, U0 + 49152)
    gateA, gateB = gates[:, :, 0:D], gates[:, :, D:2 * D]
    xn = place("xn", [P, TT, KB, P], F32, U0 + 49152)
    qz = place("qz", [P, 2, 2, T], F32, XRES)
    sc = place("sc", [P, 2, 2, 3 * P], F32, XRES + 4096)
    pT = place("pT", [P, 2, 3 * P], F32, XRES + 10240)
    osb = place("osb", [P, TT, 2, HD], F32, XRES + 13312)
    mx = place("mx", [P, 2, 2, TT], F32, XRES + 14336)
    nm = place("nm", [P, 2, 2, TT], F32, XRES + 14368)
    den = place("den", [P, 2, 2, TT], F32, XRES + 14400)
    esink = place("esink", [P, 2, 2, TT], F32, XRES + 14432)
    qk = place("qk", [P, 24, T], F32, V + 16384)
    vA = place("vA", [P, TT, HEADS * HD], F32, V + 40960)
    kB = place("kB", [P, KV, T], F32, V + 49152)
    vB = place("vB", [P, TT, KV * HD], F32, V + 53248)
    xnT = place("xnT", [P, KB, T], F32, V)
    yp = place("yp", [P, TT, KB, P], F32, V + 16384)
    y2 = place("y2", [P, TT, D], F32, V + 16384)
    h = place("h", [P, TT, KB, P], F32, V + 16384)
    acc = place("acc", [P, TT, D], F32, V)
    rowGm = place("rowGm", [P, D], F32, V)
    rowAf = place("rowAf", [P, D], F32, V + 8192)
    rowSf = place("rowSf", [P, D], F32, V + 32768)
    h2T = place("h2T", [P, KB, T], F32, V + 32768)
    dump = place("dump", [P, D], F32, V + 40960)
    xeT = place("xeT", [P, KB, P], F32, V + 32768)
    rowGf = place("rowGf", [P, D], F32, V + 32768)
    ye = place("ye", [P, D], F32, V + 40960)
    pick = place("pick", [P, TT, 2, CAP], F32, V + 49152)
    send = place("send", [P, T], F32, V + 50176)
    act = place("act", [P, 2, T], F32, V + 51200)
    actT = place("actT", [P, 2, 2, P], F32, V + 53248)
    mb = place("mb", [P, NB], F32, SM)
    condb = place("condb", [P, KB, 32], F32, SM + 2048)
    dist = place("dist", [P, 4, P], F32, SM + 4096)
    brow = place("brow", [6 * KB, P], F32, SM + 6144)
    grow = place("grow", [4 * KB, P], F32, SM + 6656)
    vrow = place("vrow", [4 * KB, P], F32, SM + 7168)
    ident = place("ident", [P, P], F32, SM + 7680)
    msum_flat = place("msum", [P, 6 * KB], F32, SM + 8192)
    msum = msum_flat[:, :].rearrange("p (v k) -> p v k", k=KB)
    badac_flat = place("badac", [P, 6 * KB], F32, SM + 8576)
    badac = badac_flat[:, :].rearrange("p (v k) -> p v k", k=KB)
    gains_flat = place("gains", [P, 4 * KB], F32, SM + 8960)
    gains = gains_flat[:, :].rearrange("p (v k) -> p v k", k=KB)
    vecs = place("vecs", [P, 4, KB], F32, SM + 9216)
    colA = place("colA", [P, KB], F32, SM + 9472)
    cc = place("cc", [P, 3, KB], F32, SM + 9536)
    ssq = place("ssq", [P, 4, TT], F32, SM + 9728)
    inv = place("inv", [P, 4, TT], F32, SM + 9760)
    rstd = place("rstd", [P, 4, TT], F32, SM + 9792)
    nslope = place("nslope", [P, HEADS + 2], F32, SM + 9824)
    sink = place("sink", [P, HEADS], F32, SM + 9920)
    sel = place("sel", [P, 1], F32, SM + 10048)
    nsink = place("nsink", [P, HEADS], F32, SM + 9984)
    iota = place("iota", [P, T], F32, SM)
    wtok = place("wtok", [P, TT, 36], F32, SM + 1024)
    rank = place("rank", [P, TT, 34], F32, SM + 1312)
    wr = place("wr", [P, KB, 36], F32, SM + 1600)
    rbias = place("rbias", [P, 36], F32, SM + 3904)
    lg = place("lg", [P, TT, 36], F32, SM + 4064)
    em = place("em", [P, TT, E], F32, SM + 4352)
    oh1 = place("oh1", [P, TT, E], F32, SM + 4608)
    oh2 = place("oh2", [P, TT, E], F32, SM + 4864)
    te = place("te", [P, TT, E], F32, SM + 5120)
    tg = place("tg", [P, TT, 4], F32, SM + 5376)
    goh = place("goh", [P, TT, 4], F32, SM + 5408)
    ex = place("ex", [P, TT, 5], F32, SM + 5440)
    m3 = place("m3", [P, 4, TT], F32, SM + 5504)
    slot = place("slot", [P, 36], F32, SM + 5536)
    wsel = place("wsel", [P, 2], F32, SM + 5824)
    desc = place("desc", [P, E], F32, SM + 5696)
    upper = place("upper", [P, P], F32, SM + 6144)
    ones = place("ones", [P, P], F32, SM + 6656)
    over = place("over", [P, TT, E], F32, SM + 7168)
    tover = place("tover", [P, TT, 2], F32, SM + 7424)
    rover = place("rover", [P, TT], F32, SM + 7456)
    cnt = place("cnt", [P, E], F32, SM + 4064)
    cum = place("cum", [P, E], F32, SM + 4192)
    whole = place("whole", [P, 16], I32, SM + 7488)
    cmpj = place("cmpj", [P, 8, E], F32, V + 40960)
    eidf = place("eidf", [P, 8], F32, SM + 7552)

    bank = [nc.alloc_psum_tensor(f"bank{i}", [P, NB], F32) for i in range(8)]

    mod_rows = nc.dram_tensor("mod_rows", [4, D], F32, kind="Internal").ap()

    ada_v = w_ada[0].rearrange("(p h k) n -> p h k n", p=P, h=2)
    in_q = w_in[0].rearrange("(q k p) n -> p q k n", p=P, q=QUARTERS)
    in_v = w_in[0].rearrange("(h k p) n -> p h k n", p=P, h=2)
    out_v = w_out[0].rearrange("(h k p) n -> p h k n", p=P, h=2)
    oA_v = w_o_moba[0].rearrange("(k p) n -> p k n", p=P)
    oB_v = w_o_swa[0].rearrange("(k p) n -> p k n", p=P)
    gate_v = w_gate[0].rearrange("e (p h k) f -> e p h (k f)", p=P, h=2)
    up_v = w_up[0].rearrange("e (p h k) f -> e p h (k f)", p=P, h=2)
    down_v = w_down[0].rearrange("e (h c p) d -> e h p c d", p=P, h=2)
    x_v = x[0].rearrange("(t p) d -> p t d", p=P)
    out_t = out[0].rearrange("(t p) d -> t p d", p=P)

    def sem(name):
        return nc.alloc_semaphore(name)

    loaded = [sem(f"slot{s}_loaded") for s in range(8)]
    x_loaded, sink_loaded, rows_loaded, c_loaded, x_again = map(sem, (
        "x_loaded", "sink_loaded", "rows_loaded", "c_loaded", "x_again"))
    rows_T, cols_ready, vecs_T, vecs_rowed = map(sem, ("rows_T", "cols_ready", "vecs_T", "vecs_rowed"))
    c_sig, cond_ready, const_ready = map(sem, ("c_sig", "cond_ready", "const_ready"))
    ssq_done, inv_ready, rstd_ready = map(sem, ("ssq_done", "inv_ready", "rstd_ready"))
    xn_ready, xT_done, xT_evac = map(sem, ("xn_ready", "xT_done", "xT_evac"))
    ada_half, ada_evac, col_done, col_evac = map(sem, ("ada_half", "ada_evac", "col_done", "col_evac"))
    colA_ready, xnT_mod, hT_ready = map(sem, ("colA_ready", "xnT_mod", "hT_ready"))
    hi_done, split_ready, split_used, block_evac = map(sem, ("hi_done", "split_ready", "split_used", "block_evac"))
    vecs_ready, rows_stored, rowm_loaded, rowf_loaded = map(sem, (
        "vecs_ready", "rows_stored", "rowm_loaded", "rowf_loaded"))
    qz_zero, qz_ready, scored, biased, nm_ready, exped = map(sem, (
        "qz_zero", "qz_ready", "scored", "biased", "nm_ready", "exped"))
    pt_done, pt_evac, pv_done, o_scaled, ot_done, ot_evac = map(sem, (
        "pt_done", "pt_evac", "pv_done", "o_scaled", "ot_done", "ot_evac"))
    gate_ready = sem("gate_ready")
    oT_split, gated, y_added, yT_done, yT_hi, yT_ready = map(sem, (
        "oT_split", "gated", "y_added", "yT_done", "yT_hi", "yT_ready"))
    y2_evac, x2_ready, h_ready, h2T_done, h2T_evac = map(sem, (
        "y2_evac", "x2_ready", "h_ready", "h2T_done", "h2T_evac"))
    router_loaded, rconst_ready, logits_done, ex_in, ex_done, hot_ready, rank_done, tables_ready = map(sem, (
        "router_loaded", "rconst_ready", "logits_done", "ex_in", "ex_done", "hot_ready", "rank_done",
        "tables_ready"))
    acc_zero, picked, slots_done, slots_evac, got_done, got_evac = map(sem, (
        "acc_zero", "picked", "slots_done", "slots_evac", "got_done", "got_evac"))
    gu_half, sig_done, act_ready, aT_done, aT_evac = map(sem, (
        "gu_half", "sig_done", "act_ready", "aT_done", "aT_evac"))
    y_done, y_evac, send_ready, comb_done, comb_added = map(sem, (
        "y_done", "y_evac", "send_ready", "comb_done", "comb_added"))
    ov_go, ov_pick, ov_got, ov_in, ov_gu, ov_sig, ov_act, ov_aT, ov_aTe, ov_y, ov_ye, ov_comb = (
        sem(f"over_{n}") for n in ("go", "pick", "got", "in", "gu", "sig", "act", "aT", "aTe", "y", "ye", "comb"))
    acc_final, fin_ready, stored = sem("acc_final"), sem("fin_ready"), sem("stored")

    FRONT_USES = [25, 25, 24, 24, 0, 0, 0, 0]
    ORDER = [2, 3, 4, 5, 6, 7, 0, 1]
    C_BLOCKS, C_KV = 20, 44
    C_GATES, C_O = 50, 82
    U_BLOCKS = 2 * KB
    U_GATES = U_BLOCKS + 7 * KB
    U_IN_END = U_GATES + 8 * KB
    U_O_END = U_IN_END + 2 * DB * 8
    U_END = U_O_END + DB * KB
    CREDIT = SPLITS

    def slot4(s):
        return ring[:, s, :].rearrange("p (k n) -> p k n", k=8)

    def e_chunk(m):
        return ORDER[m % 8], m // 8 + 1

    def front(c):
        return c % 4, 16 * (c // 4 + 1)

    block = nc.Block()
    block.__enter__()

    @block.sync
    def _(sp):
        def load(s, src):
            shape4 = len(src.shape) == 3
            dst = slot4(s) if shape4 and src.shape[1] == 8 else (
                ring[:, s, :].rearrange("p (c d) -> p c d", c=2) if shape4 else ring[:, s, :])
            sp.dma_start(dst, src).then_inc(loaded[s], 16)

        def cols(v, hf, at):
            return v[:, hf, :, bass.ds(at, NB)]

        sp.dma_start(xres[:, :, :], x_v).then_inc(x_loaded, 16)
        for n in range(C_BLOCKS):
            q, part = n // 5, n % 5
            if n >= 4:
                q0, part0 = (n - 4) // 5, (n - 4) % 5
                if part0 < 4:
                    sp.wait_ge(ada_half, 4 * q0 + part0 + 1)
                else:
                    sp.wait_ge(split_ready, 8 * (q0 + 1))
            if part < 4:
                load(n % 4, cols(ada_v, part % 2, (part // 2) * D + q * NB))
            else:
                sp.dma_start(ring[:, n % 4, :].rearrange("p (k n) -> p k n", k=4),
                             in_q[:, q, :, COL_QA:COL_QA + 2 * NB]).then_inc(loaded[n % 4], 16)

        def in_block(n, col, sa, ada_to, split_to, last_split=True):
            for q in range(2):
                sp.wait_ge(ada_half, ada_to + q)
                load(sa + q, cols(ada_v, q, n * NB))
            for q in range(2):
                if last_split:
                    sp.wait_ge(split_ready, split_to + 8 * q)
                load(2 - sa + q, cols(in_v, q, col))

        for q in range(2):
            sp.wait_ge(ada_half, 14 + q)
            load(q, cols(ada_v, q, ADA_FIRST * NB))
        sp.wait_ge(ada_half, 16)
        load(2, cols(in_v, 0, COL_KA))
        sp.wait_ge(split_ready, U_BLOCKS)
        load(3, cols(in_v, 1, COL_KA))
        for b0, n, col in ((1, 1, COL_KA + NB), (2, 2, COL_QB), (4, 2, COL_VA)):
            with sp.Fori(b0, b0 + n) as b:
                in_block(b + ADA_FIRST, b * NB + (col - b0 * NB), 0, b * 2 + (2 * ADA_FIRST - 1),
                         b * 16 + (U_BLOCKS - 8))
        for n in range(6):
            b = 6
            if n < 2:
                sp.wait_ge(ada_half, 2 * (ADA_FIRST + b) - 1 + n)
                load(n, cols(ada_v, n, (ADA_FIRST + b) * NB))
            elif n < 4:
                sp.wait_ge(split_ready, U_BLOCKS + 16 * (b - 1) + 8 * (n - 1))
                load(n, cols(in_v, n - 2, COL_KVB))
            else:
                sp.wait_ge(ada_half, 2 * (ADA_FIRST + b) + n - 3)
                load(n - 4, cols(ada_v, n - 4, (ADA_FIRST + b + 1) * NB))
        for q in range(2):
            sp.wait_ge(split_ready, U_GATES - 8 + 8 * q)
            load(2 + q, cols(ada_v, q, 16 * NB))
        for q in range(2):
            sp.wait_ge(ada_half, 31 + q)
            load(q, cols(in_v, q, COL_G))
        with sp.Fori(1, 8) as g:
            in_block(g + 16, g * NB + COL_G, 2, g * 2 + 31, g * 16 + (U_GATES - 8))
        for n in range(16):
            slot_n = (2 + n) % 4
            if n < 2:
                sp.wait_ge(ada_half, 2 * ADA_BLOCKS - 1 + n)
            else:
                sp.wait_ge(split_ready, U_IN_END + 8 * (n - 3))
            if n < 8:
                v = oA_v if n % 2 == 0 else oB_v
                load(slot_n, v[:, :, (n // 2) * NB:(n // 2 + 1) * NB])
            else:
                load(slot_n, cols(out_v, n % 2, ((n - 8) // 2) * NB))

        def expert_chunk(e, q):
            if q < 4:
                return (gate_v if q % 2 == 0 else up_v)[e, :, q // 2, :]
            return down_v[e, q - 4, :, :, :]

        def used(pair2, m):
            r, q = m // 12, m % 12
            if q < 8:
                sp.wait_ge(gu_half, pair2 * 4 + (4 * r + q // 2 + 1))
            else:
                sp.wait_ge(y_done, pair2 * 4 + (4 * r + 4))

        def expert_step(i, first):
            for m in range(24):
                s, _ = e_chunk(m)
                if m >= 8:
                    used(i * 2, m - 8)
                elif not first:
                    used(i * 2 - 2, m + 16)
                elif m < 2:
                    sp.wait_ge(split_ready, 8 * (47 + m))
                elif m < 6:
                    sp.wait_ge(split_used, U_END + CREDIT)
                else:
                    sp.wait_ge(split_ready, 8 * (43 + m))
                r, q = m // 12, m % 12
                e, part = (q // 4, q % 4) if q < 8 else ((q - 8) // 2, 4 + (q - 8) % 2)
                load(s, expert_chunk(i * 4 + (2 * r + e), part))

        expert_step(0, True)
        with sp.Fori(1, E // 4) as i:
            expert_step(i, False)

        sp.wait_ge(tables_ready, 2)
        n_over = sp.value_load(whole[0:1, 8:9], min_val=0, max_val=MAX_OVER)
        with sp.If(n_over > 0):
            sp.wait_ge(y_done, 4 * E // 2)
            with sp.Fori(0, n_over) as j:
                sp.wait_ge(ov_go, j + 1)
                e = sp.value_load(whole[0:1, bass.ds(j, 1)], min_val=0, max_val=E - 1)
                for q in range(6):
                    load(ORDER[q], expert_chunk(e, q))

        for t in range(TT):
            sp.wait_ge(fin_ready, t + 1)
            sp.dma_start(out_t[t], xres[:, t, :]).then_inc(stored, 16)
        sp.wait_ge(stored, 16 * TT)

    @block.gpsimd
    def _(pool):
        nc.gpsimd.memset(ident[:, :], 0.0)
        nc.gpsimd.memset(nslope[:, HEADS:HEADS + 2], 0.0)
        for n in range(HEADS):
            nc.gpsimd.memset(nslope[:, n:n + 1], -8.0 * 2.0 ** (-8.0 * (n + 1) / HEADS))
        nc.gpsimd.iota(dist[:, 0, :], pattern=[[-1, P]], base=P, channel_multiplier=1,
                       allow_small_or_imprecise_dtypes=True)
        nc.gpsimd.iota(dist[:, 1, :], pattern=[[-1, P]], base=0, channel_multiplier=1,
                       allow_small_or_imprecise_dtypes=True)
        nc.gpsimd.iota(dist[:, 2, :], pattern=[[-1, P]], base=0, channel_multiplier=1,
                       allow_small_or_imprecise_dtypes=True)
        nc.gpsimd.iota(dist[:, 3, :], pattern=[[-1, P]], base=P, channel_multiplier=1,
                       allow_small_or_imprecise_dtypes=True)
        pool.drain()
        nc.gpsimd.affine_select(out=ident[:, :], in_=ident[:, :], compare_op=ALU.not_equal, fill=1.0, base=0,
                                pattern=[[-1, P]], channel_multiplier=1)
        for n in (1, 2):
            nc.gpsimd.affine_select(out=dist[:, n, :], in_=dist[:, n, :], compare_op=ALU.is_ge, fill=MASKED,
                                    base=0, pattern=[[-1, P]], channel_multiplier=1)
        nc.gpsimd.affine_select(out=dist[:, 3, :], in_=dist[:, 3, :], compare_op=ALU.is_gt, fill=MASKED,
                                base=0, pattern=[[1, P]], channel_multiplier=-1)
        pool.drain().then_inc(const_ready, 1)
        pool.dma_start(sink[:, :], swa_sinks[0:1, :].broadcast_to([P, HEADS])).then_inc(sink_loaded, 16)

        pool.wait_ge(xn_ready, TT)
        nc.gpsimd.memset(qz[:, :, :, :], 0.0)
        pool.drain()
        pool.wait_ge(block_evac, 8)

        def queries(R, r, blk):
            pool.wait_ge(scored, R + 1)
            for hh in range(2):
                nc.gpsimd.tensor_copy(qz[HD * hh:HD * hh + HD, r % 2, hh, :],
                                      qk[HD * hh:HD * hh + HD, bass.ds(blk, 1), :].rearrange("p a t -> p (a t)"))\
                    .then_inc(qz_ready, 1)

        with pool.Fori(0, 4) as i:
            for r in range(4):
                queries(i * 4 + r, r, i * 2 + (r // 2 + (0 if r % 2 == 0 else 16)))
        queries(PAIRS * 2, 0, PAIRS)

        pool.wait_ge(vecs_rowed, 1)
        pool.dma_start(mod_rows.rearrange("v (k p) -> (v k) p", p=P), vrow[:, :]).then_inc(rows_stored, 16)
        pool.wait_ge(o_scaled, 17)
        pool.wait_ge(ot_evac, 17)
        pool.dma_start(xres[:, :, :], x_v).then_inc(x_again, 16)
        nc.gpsimd.iota(iota[:, :], pattern=[[1, T]], base=0, channel_multiplier=0,
                       allow_small_or_imprecise_dtypes=True)
        nc.gpsimd.iota(desc[:, :], pattern=[[-1, E]], base=E, channel_multiplier=0,
                       allow_small_or_imprecise_dtypes=True)
        nc.gpsimd.memset(wtok[:, :, :], 0.0)
        nc.gpsimd.memset(rank[:, :, :], -1.0)
        nc.gpsimd.memset(ones[:, :], 1.0)
        nc.gpsimd.memset(upper[:, :], 1.0)
        pool.drain()
        for t in range(TT):
            nc.gpsimd.iota(wtok[:, t, 34:35], pattern=[[0, 1]], base=t * P, channel_multiplier=1,
                           allow_small_or_imprecise_dtypes=True)
        nc.gpsimd.affine_select(out=upper[:, :], in_=upper[:, :], compare_op=ALU.is_gt, fill=0.0, base=0,
                                pattern=[[1, P]], channel_multiplier=-1)
        pool.drain().then_inc(rconst_ready, 1)
        pool.dma_start(wr[:, :, 0:GROUPS], w_router_group[0].rearrange("(p k) n -> p k n", k=KB))\
            .then_inc(router_loaded, 16)
        pool.dma_start(wr[:, :, GROUPS:36], w_router_expert[0].rearrange("(p k) n -> p k n", k=KB))\
            .then_inc(router_loaded, 16)
        pool.dma_start(rbias[:, 0:GROUPS], b_router_group[0:1, :].broadcast_to([P, GROUPS])).then_inc(router_loaded, 16)
        pool.dma_start(rbias[:, GROUPS:36], b_router_expert[0:1, :].broadcast_to([P, E])).then_inc(router_loaded, 16)

        for nb in range(DB):
            pool.wait_ge(gated, nb + 1)
            for t in range(TT):
                nc.gpsimd.tensor_tensor(
                    yp[:, t, nb * 4:(nb + 1) * 4, :],
                    gateA[:, t, nb * NB:(nb + 1) * NB].rearrange("p (k q) -> p k q", k=4),
                    gateB[:, t, nb * NB:(nb + 1) * NB].rearrange("p (k q) -> p k q", k=4), ALU.add)\
                    .then_inc(y_added, 1)
        pool.wait_ge(y_added, DB * TT)
        pool.wait_ge(rows_stored, 16)
        for n, row in ((0, rowGm), (2, rowAf), (1, rowSf)):
            pool.dma_start(row[:, :], mod_rows[n:n + 1, :].broadcast_to([P, D])).then_inc(rowm_loaded, 16)
        pool.wait_ge(h_ready, TT)
        nc.gpsimd.memset(acc[:, :, :], 0.0).then_inc(acc_zero, 1)
        pool.wait_ge(acc_final, 1)
        pool.dma_start(rowGf[:, :], mod_rows[3:4, :].broadcast_to([P, D])).then_inc(rowf_loaded, 16)

    @block.scalar
    def _(sc_e):
        a = nc.scalar
        a_copy = lambda o, i_: a.activation(o, i_, ACT.Copy)

        def squares(n, src, buf):
            for t in range(TT):
                last = a.activation(buf, src[:, t, :], ACT.Square, accum_out=ssq[:, n, t:t + 1])
                sc_e.drain()
            last = sc_e.drain().then_inc(ssq_done, 1)
            sc_e.wait_ge(inv_ready, n + 1)
            a.activation(rstd[:, n, :], inv[:, n, :], ACT.Sqrt).then_inc(rstd_ready, 1)

        sc_e.dma_start(cc[:, 0, :], c[0].rearrange("(p k) -> p k", k=KB)).then_inc(c_loaded, 16)
        sc_e.dma_start(brow[:, :], b_ada[0].rearrange("(k p) -> k p", p=P)).then_inc(rows_loaded, 16)
        for n, g in enumerate((g_pre_mix, g_post_mix, g_pre_ffn, g_post_ffn)):
            sc_e.dma_start(grow[KB * n:KB * (n + 1), :], g[0].rearrange("(k p) -> k p", p=P))\
                .then_inc(rows_loaded, 16)
        sc_e.wait_ge(c_loaded, 16)
        a.activation(cc[:, 1, :], cc[:, 0, :], ACT.Sigmoid).then_inc(c_sig, 1)
        sc_e.wait_ge(x_loaded, 16)
        squares(0, xres, gateA[:, 0, :])

        def ada_out(m):
            sc_e.wait_ge(ada_half, m * 2 + 2)
            sc_e.wait_ge(col_done, m + 1)
            a_copy(mb[:, :], bank[2][:, :]).then_inc(ada_evac, 1)

        def col_out(m, n):
            sc_e.wait_ge(col_done, m + 2)
            a_copy(msum_flat[:, bass.ds(n * 4, 4)], bank[2][:, 0:4]).then_inc(col_evac, 1)

        sc_e.sem_inc(col_evac, 1)
        for q in range(QUARTERS):
            for part in range(2):
                ada_out(2 * q + part)
                col_out(2 * q + part, QUARTERS * part + q)
            sc_e.wait_ge(colA_ready, q + 1)
            for k in range(4 * q, 4 * q + 4):
                if k % 4 == 0:
                    sc_e.wait_ge(xT_evac, 8)
                a.activation(xnT[:, k, :], xnT[:, k, :], ACT.Identity, bias=msum[:, 0, k:k + 1],
                             scale=colA[:, k:k + 1]).then_inc(xnT_mod, 1)

        def block_out(u_end, dst, banks=(0, 1), func=ACT.Copy):
            sc_e.wait_ge(split_used, u_end + CREDIT)
            for t in range(2):
                last = a.activation(dst(t), bank[banks[t]][:, :], func)
            last.then_inc(block_evac, 1)

        for n in range(2):
            block_out(U_BLOCKS, lambda t: qk[:, 4 * n + 2 * t:4 * n + 2 * t + 2, :].rearrange("p a t -> p (a t)"),
                      banks=((0, 1), (3, 4))[n])
        with sc_e.Fori(0, 4) as b:
            ada_out(b + ADA_FIRST)
            col_out(b + ADA_FIRST, b + ADA_FIRST)
            block_out(b * KB + (U_BLOCKS + KB), lambda t: qk[:, bass.ds(b * 4 + (8 + 2 * t), 2), :]
                      .rearrange("p a t -> p (a t)"))
        for n in range(2):
            ada_out(n + 4 + ADA_FIRST)
            col_out(n + 4 + ADA_FIRST, n + 4 + ADA_FIRST)
            block_out(U_BLOCKS + (5 + n) * KB, lambda t: vA[:, t, n * NB:(n + 1) * NB])
        for m in (14, 15):
            ada_out(m)
            col_out(m, m)
        sc_e.wait_ge(split_used, U_GATES + CREDIT)
        for hf in range(2):
            for par in range(2):
                a_copy(kB[HD * hf:HD * hf + HD, par:KV:2, :],
                       bank[0][HD * par:HD * par + HD, :].rearrange("p (b t) -> p b t", b=2))
        a_copy(vB[:, :, :], bank[1][:, :].rearrange("p (t n) -> p t n", t=TT)).then_inc(block_evac, 1)

        sc_e.sem_inc(pt_evac, 1)
        sc_e.wait_ge(sink_loaded, 16)
        sc_e.sem_inc(ot_evac, 1)
        sc_e.sem_inc(aT_evac, 1)
        sc_e.sem_inc(y_evac, 2)

        def exps(R, r, i):
            b = r % 2
            sc_e.wait_ge(nm_ready, R + 1)
            t1, t0 = (slice(0, 256), slice(256, 384)) if b == 0 else (slice(128, 384), slice(0, 128))
            for hh in range(2):
                for t, cut in ((0, t0), (1, t1)):
                    last = a.activation(sc[:, b, hh, cut], sc[:, b, hh, cut], ACT.Exp, scale=0.125,
                                        bias=nm[:, b, hh, t:t + 1], accum_out=den[:, b, hh, t:t + 1])
                if b == 1:
                    head = i * 4 + ((r // 2) * 2 + hh)
                    a.activation(esink[:, b, hh, :], nm[:, b, hh, :], ACT.Exp,
                                        bias=sink[:, bass.ds(head, 1)])
            sc_e.drain().then_inc(exped, 1)

        def pt_out(R, hh):
            sc_e.wait_ge(pt_done, R * 2 + (hh + 3))
            sc_e.wait_ge(pv_done, R * 2 + hh)
            a_copy(pT[:, hh, :], bank[5][:, 0:3 * P]).then_inc(pt_evac, 1)

        def ot_out(R, r, i):
            blk = i * 2 + (r // 2 + (0 if r % 2 == 0 else 16))
            sc_e.wait_ge(ot_done, R + 2)
            a_copy(qk[:, bass.ds(blk, 1), :].rearrange("p a t -> p (a t)"), bank[7][:, 0:T]).then_inc(ot_evac, 1)

        exps(0, 0, 0)
        with sc_e.Fori(0, 4) as i:
            for r in range(4):
                R = i * 4 + r
                for hh in range(2):
                    pt_out(R, hh)
                    if hh == 0 and r % 2 == 0:
                        ada_out(i * 2 + (16 + r // 2))
                exps(i * 4 + (r + 1), r + 1, i)
                if r % 2 == 0:
                    col_out(i * 2 + (16 + r // 2), i * 2 + (16 + r // 2))
                ot_out(R, r, i)
                if r % 2 == 1:
                    sc_e.wait_ge(split_used, i * 32 + (U_GATES + 16 * (r // 2 + 1) + CREDIT))
                    for t in range(TT):
                        last = a.activation(gates[:, t, bass.ds(i * 2 * NB + (r // 2) * NB, NB)], bank[t][:, :],
                                            ACT.Copy)
                    last.then_inc(block_evac, 1)
        sc_e.wait_ge(vecs_T, 1)
        a_copy(vrow[:, :], bank[2][0:4 * KB, 0:P]).then_inc(vecs_rowed, 1)
        sc_e.wait_ge(block_evac, 17)
        for nb in range(DB):
            for t in range(TT):
                cut = gates[:, t, :].rearrange("p (m n) -> p m n", m=2)[:, :, nb * NB:(nb + 1) * NB]
                last = a.activation(cut, cut, ACT.Sigmoid)
            last.then_inc(gate_ready, 1)

        for g in range(8):
            t, kq = g // 4, g % 4
            sc_e.wait_ge(yT_done, g + 1)
            a_copy(hT_hi[:, 4 * kq:4 * kq + 4, t * P:(t + 1) * P],
                   bank[g % 4][:, :].rearrange("p (k q) -> p k q", k=4)).then_inc(yT_hi, 1)
        for nb in range(DB):
            sc_e.wait_ge(split_used, U_O_END + 16 * (nb + 1) + CREDIT)
            for t in range(TT):
                last = a_copy(y2[:, t, nb * NB:(nb + 1) * NB], bank[4 + 2 * (nb % 2) + t][:, :])
            last.then_inc(y2_evac, 1)
        sc_e.wait_ge(y2_evac, DB)
        squares(1, y2, dump[:, :])
        sc_e.wait_ge(x2_ready, 1)
        squares(2, xres, dump[:, :])
        for g in range(8):
            t, kq = g // 4, g % 4
            sc_e.wait_ge(h2T_done, g + 1)
            a_copy(h2T[:, 4 * kq:4 * kq + 4, t * P:(t + 1) * P],
                   bank[g % 4][:, :].rearrange("p (k q) -> p k q", k=4)).then_inc(h2T_evac, 1)
        sc_e.wait_ge(ex_in, 1)
        a.activation(ex[:, :, :], ex[:, :, :], ACT.Exp).then_inc(ex_done, 1)

        def gather_out(r1):
            sc_e.wait_ge(slots_done, r1 + 1)
            a_copy(slot[:, :], bank[7][:, 0:36]).then_inc(slots_evac, 1)
            for g in range(4):
                sc_e.wait_ge(got_done, r1 * 4 + (g + 1))
                a_copy(xeT[:, 4 * g:4 * g + 4, :], bank[7][:, :].rearrange("p (k s) -> p k s", k=4))\
                    .then_inc(got_evac, 1)

        gather_out(0)

        def pair(r):
            for e in range(2):
                sc_e.wait_ge(gu_half, r * 4 + 2 * (e + 1))
                sc_e.wait_ge(aT_done, r + 1)
                a.activation(act[:, e, :], bank[e][:, 0:T], ACT.Sigmoid).then_inc(sig_done, 1)
            gather_out(r + 1)
            sc_e.wait_ge(aT_done, r + 2)
            a_copy(actT[:, :, :, :].rearrange("p e c s -> p (e c s)"), bank[2][:, :]).then_inc(aT_evac, 1)
            for nb in range(DB):
                sc_e.wait_ge(y_done, r * 4 + (nb + 1))
                sc_e.wait_ge(comb_done, r * 8 + (2 * nb + 2))
                a_copy(ye[:, nb * NB:(nb + 1) * NB], bank[3 + nb % 2][:, :]).then_inc(y_evac, 1)

        with sc_e.Fori(0, E // 4) as i:
            for x2 in range(2):
                pair(i * 2 + x2)

        sc_e.wait_ge(tables_ready, 2)
        n_over = sc_e.value_load(whole[0:1, 8:9], min_val=0, max_val=MAX_OVER)
        with sc_e.If(n_over > 0):
            with sc_e.Fori(0, n_over) as j:
                sc_e.wait_ge(ov_got, j + 1)
                a_copy(slot[0:CAP, 0:2], bank[7][0:CAP, 0:2])
                for n in range(2):
                    last = a_copy(xeT[:, 8 * n:8 * n + 8, 0:CAP],
                                  bank[5 + n][:, :].rearrange("p (k s) -> p k s", k=8))
                last.then_inc(ov_in, 1)
                sc_e.wait_ge(ov_gu, j + 1)
                a.activation(act[:, 0, :], bank[0][:, 0:T], ACT.Sigmoid).then_inc(ov_sig, 1)
                sc_e.wait_ge(ov_aT, j + 1)
                a_copy(actT[:, 0, :, :].rearrange("p c s -> p (c s)"), bank[2][:, 0:T]).then_inc(ov_aTe, 1)
                sc_e.wait_ge(ov_y, j + 1)
                for nb in range(DB):
                    last = a_copy(ye[0:CAP, nb * NB:(nb + 1) * NB], bank[3 + nb][0:CAP, :])
                last.then_inc(ov_ye, 1)
        sc_e.wait_ge(acc_final, 1)
        squares(3, acc, dump[:, :])

    @block.tensor
    def _(pe):
        mm, tr = nc.tensor.matmul, nc.tensor.transpose
        pe.sem_inc(split_used, CREDIT)
        pe.sem_inc(scored, 2)
        pe.sem_inc(pt_done, 2)
        pe.sem_inc(pv_done, 1)
        pe.sem_inc(ot_done, 1)
        pe.sem_inc(aT_done, 1)
        pe.sem_inc(col_done, 1)
        pe.sem_inc(comb_done, 8)

        def ada(m, at):
            pe.wait_ge(col_evac, m + 1)
            for hf, (s, count) in enumerate(at):
                pe.wait_ge(loaded[s], count)
                for kk in range(8):
                    k = hf * 8 + kk
                    g = kk % 4
                    last = mm(bank[2][32 * g:32 * g + 32, :], condb[:, k, :], ring[:, s, kk * NB:(kk + 1) * NB],
                              start=(k < 4), stop=(k >= 12))
                last.then_inc(ada_half, 1)

        def col(m):
            pe.wait_ge(ada_evac, m + 1)
            for q in range(4):
                last = mm(bank[2][:, q:q + 1], mb[:, q * P:(q + 1) * P], sel[:, :], start=True, stop=True)
            last.then_inc(col_done, 1)

        def split_mm(o_of, hi, lo, k, b, start, stop):
            for t in range(TT):
                cut = slice(t * P, (t + 1) * P)
                mm(o_of(t), hi[:, k, cut], w_hi[:, b, :], start=start, stop=False)
                mm(o_of(t), hi[:, k, cut], w_lo[:, b, :], start=False, stop=False)
                last = mm(o_of(t), lo[:, k, cut], w_hi[:, b, :], start=False, stop=stop)
            last.then_inc(split_used, 1)

        def split_mm_T(outs, k, b, start, stop):
            for blk in range(4):
                o = outs[blk // 2][:, (blk % 2) * T:(blk % 2 + 1) * T]
                cut = slice(blk * P, (blk + 1) * P)
                mm(o, w_hi[:, b, cut], hT_hi[:, k, :], start=start and blk % 2 == 0, stop=False,
                   skip_group_check=True)
                mm(o, w_hi[:, b, cut], hT_lo[:, k, :], start=False, stop=False, skip_group_check=True)
                last = mm(o, w_lo[:, b, cut], hT_hi[:, k, :], start=False, stop=stop, skip_group_check=True)
            last.then_inc(split_used, 1)

        pe.wait_ge(const_ready, 1)
        pe.wait_ge(rows_loaded, 80)
        tr(bank[7][:, 0:6 * KB], brow[:, :], ident[0:6 * KB, 0:6 * KB])
        tr(bank[7][:, P:P + 4 * KB], grow[:, :], ident[0:4 * KB, 0:4 * KB]).then_inc(rows_T, 1)
        pe.wait_ge(cond_ready, 1)
        for q in range(QUARTERS):
            for part in range(2):
                ada(2 * q + part, [front(5 * q + 2 * part), front(5 * q + 2 * part + 1)])
                if q == 0 and part == 0:
                    for g in range(8):
                        t, kq = g // 4, g % 4
                        if g % 4 == 0:
                            pe.wait_ge(xn_ready, t + 1)
                        if g >= 2:
                            pe.wait_ge(xT_evac, g - 1)
                        for n in range(4):
                            last = tr(bank[5 + g % 2][:, n * P:(n + 1) * P], xn[:, t, 4 * kq + n, :], ident[:, :])
                        last.then_inc(xT_done, 1)
                col(2 * q + part)
            pe.wait_ge(hT_ready, q + 1)
            for n in range(8):
                pe.wait_ge(split_ready, 8 * q + n + 1)
                k = 4 * q + n // 2
                split_mm_T((bank[0:2], bank[3:5])[n % 2], k, n % SPLITS, k == 0, k == KB - 1)

        def in_steps(u, k0, k1, transposed):
            for k in range(k0, k1):
                pe.wait_ge(split_ready, u + (k + 1))
                if transposed:
                    split_mm_T(bank[0:2], k, k % SPLITS, k == 0, k == KB - 1)
                else:
                    split_mm(lambda t: bank[t][:, :], hT_hi, hT_lo, k, k % SPLITS, k == 0, k == KB - 1)

        def in_block(b, transposed):
            ada(b + ADA_FIRST, [(0, b * 16 + 16 * (C_BLOCKS // 4 + 1)), (1, b * 16 + 16 * (C_BLOCKS // 4 + 1))])
            pe.wait_ge(block_evac, b + 2)
            in_steps(b * KB + U_BLOCKS, 0, 8, transposed)
            col(b + ADA_FIRST)
            in_steps(b * KB + U_BLOCKS, 8, KB, transposed)

        with pe.Fori(0, 4) as b:
            in_block(b, True)
        with pe.Fori(4, 6) as b:
            in_block(b, False)
        ada(14, [front(C_KV), front(C_KV + 1)])
        pe.wait_ge(block_evac, 8)
        for k in range(KB):
            if k == 8:
                col(14)
            pe.wait_ge(split_ready, U_BLOCKS + 6 * KB + k + 1)
            b = k % SPLITS
            for blk in range(2):
                o = bank[0][:, blk * T:(blk + 1) * T]
                cut = slice(blk * P, (blk + 1) * P)
                for n, (w, hh) in enumerate(((w_hi, hT_hi), (w_hi, hT_lo), (w_lo, hT_hi))):
                    mm(o, w[:, b, cut], hh[:, k, :], start=(k == 0 and blk == 0 and n == 0), stop=(k == KB - 1),
                       skip_group_check=True)
            for t in range(TT):
                o = bank[1][:, t * T:(t + 1) * T]
                cut = slice(t * P, (t + 1) * P)
                for n, (w, hh) in enumerate(((w_hi, hT_hi), (w_hi, hT_lo), (w_lo, hT_hi))):
                    last = mm(o, hh[:, k, cut], w[:, b, 2 * P:4 * P], start=(k == 0 and t == 0 and n == 0),
                              stop=(k == KB - 1), skip_group_check=True)
            last.then_inc(split_used, 1)
        ada(15, [front(C_KV + 4), front(C_KV + 5)])
        col(15)

        SB = (3, 4)

        def scores(R, r, i):
            b = r % 2
            pe.wait_ge(qz_ready, R * 2 + 2)
            pe.wait_ge(biased, R + 1)
            for hh in range(2):
                o = bank[SB[hh]]
                q0, q1 = qz[:, b, hh, 0:P], qz[:, b, hh, P:T]
                if b == 0:
                    kk = i * 2 + (8 + r // 2)
                    key = lambda lo_, hi_: qk[:, bass.ds(kk, 1), lo_:hi_].rearrange("p a t -> p (a t)")
                    mm(o[:, 0:T], q1, key(0, T), start=True, stop=True)
                    last = mm(o[:, T:3 * P], q0, key(0, P), start=True, stop=True)
                else:
                    key = lambda lo_, hi_: kB[:, bass.ds(i, 1), lo_:hi_].rearrange("p a t -> p (a t)")
                    mm(o[:, 0:P], q0, key(0, P), start=True, stop=True)
                    mm(o[:, P:T], q1, key(P, T), start=True, stop=True)
                    last = mm(o[:, T:3 * P], q1, key(0, P), start=True, stop=True)
            last.then_inc(scored, 1)

        def transposed_p(R, r, hh):
            if hh == 0:
                pe.wait_ge(exped, R + 1)
            pe.wait_ge(pt_evac, R * 2 + (hh + 1))
            for n in range(3):
                last = tr(bank[5][:, n * P:(n + 1) * P], sc[:, r % 2, hh, n * P:(n + 1) * P], ident[:, :])
            last.then_inc(pt_done, 1)

        def pv(R, r, i, hh):
            b = r % 2
            pe.wait_ge(pt_evac, R * 2 + (hh + 2))
            pe.wait_ge(o_scaled, R + 1)
            if b == 0:
                at = i * (4 * HD) + ((r // 2) * 2 * HD + hh * HD)
                val = lambda t: vA[:, t, bass.ds(at, HD)]
                cuts = ((0, ((2, 0),)), (1, ((0, 0), (1, 1))))
            else:
                val = lambda t: vB[:, t, bass.ds(i * HD, HD)]
                cuts = ((0, ((0, 0),)), (1, ((1, 1), (2, 0))))
            for t, parts in cuts:
                o = bank[6][:, (hh * 2 + t) * HD:(hh * 2 + t + 1) * HD]
                for n, (pb, kt) in enumerate(parts):
                    last = mm(o, pT[:, hh, pb * P:(pb + 1) * P], val(kt), start=(n == 0),
                              stop=(n == len(parts) - 1))
            last.then_inc(pv_done, 1)

        def transposed_o(R):
            pe.wait_ge(o_scaled, R + 2)
            pe.wait_ge(ot_evac, R + 1)
            for t in range(TT):
                last = tr(bank[7][:, t * P:(t + 1) * P], osb[:, t, :, :].rearrange("p h d -> p (h d)"), ident[:, :])
            last.then_inc(ot_done, 1)

        scores(0, 0, 0)
        with pe.Fori(0, 4) as i:
            for half in range(2):
                m = i * 2 + (16 + half)
                uses_g = i * 32 + 16 * (half + 1 + C_GATES // 4)
                u = i * 32 + (U_GATES + 16 * half)
                ada(m, [(2, uses_g), (3, uses_g)])
                pe.wait_ge(block_evac, i * 2 + (9 + half))
                for w in range(2):
                    r = 2 * half + w
                    R = i * 4 + r
                    transposed_p(R, r, 0)
                    in_steps(u, 8 * w, 8 * w + 2, False)
                    transposed_p(R, r, 1)
                    pv(R, r, i, 0)
                    in_steps(u, 8 * w + 2, 8 * w + 3, False)
                    scores(R + 1, r + 1, i)
                    in_steps(u, 8 * w + 3, 8 * w + 4, False)
                    pv(R, r, i, 1)
                    if w == 0:
                        col(m)
                    in_steps(u, 8 * w + 4, 8 * w + 7, False)
                    transposed_o(R)
                    in_steps(u, 8 * w + 7, 8 * w + 8, False)

        pe.wait_ge(vecs_ready, 1)
        pe.wait_ge(col_evac, ADA_BLOCKS + 1)
        tr(bank[2][0:4 * KB, 0:P], vecs[:, :, :].rearrange("p v k -> p (v k)"), ident[:, :]).then_inc(vecs_T, 1)
        pe.wait_ge(vecs_rowed, 1)
        pe.wait_ge(block_evac, 17)
        pe.wait_ge(ot_evac, 17)
        for nb in range(DB):
            if nb >= 2:
                pe.wait_ge(gated, nb - 1)
            for m in range(2):
                pe.wait_ge(oT_split, m + 1)
                outs = bank[4 * (nb % 2) + 2 * m:4 * (nb % 2) + 2 * m + 2]
                for kk in range(8):
                    pe.wait_ge(split_ready, U_IN_END + nb * 16 + m * 8 + kk + 1)
                    b = kk % SPLITS
                    split_mm(lambda t: outs[t][:, :], hT_hi, hT_lo, m * 8 + kk, b, kk == 0, kk == 7)
        pe.wait_ge(y_added, DB * TT)
        pe.wait_ge(gated, DB)
        for g in range(8):
            t, kq = g // 4, g % 4
            if g >= 4:
                pe.wait_ge(yT_ready, g - 3)
            for q in range(4):
                last = tr(bank[g % 4][:, q * P:(q + 1) * P], yp[:, t, 4 * kq + q, :], ident[:, :])
            last.then_inc(yT_done, 1)
        pe.wait_ge(yT_ready, 8)
        for nb in range(DB):
            if nb >= 2:
                pe.wait_ge(y2_evac, nb - 1)
            for k in range(KB):
                pe.wait_ge(split_ready, U_O_END + nb * 16 + k + 1)
                split_mm(lambda t: bank[4 + 2 * (nb % 2) + t][:, :], hT_hi, hT_lo, k, k % SPLITS, k == 0,
                         k == KB - 1)

        for g in range(8):
            t, kq = g // 4, g % 4
            if g == 0:
                pe.wait_ge(h_ready, TT)
            if g >= 4:
                pe.wait_ge(h2T_evac, g - 3)
            for q in range(4):
                last = tr(bank[g % 4][:, q * P:(q + 1) * P], h[:, t, 4 * kq + q, :], ident[:, :])
            last.then_inc(h2T_done, 1)
        pe.wait_ge(h2T_evac, 8)
        pe.wait_ge(router_loaded, 64)
        pe.wait_ge(y2_evac, DB)
        for t in range(TT):
            for k in range(KB):
                last = mm(bank[4][:, t * 64:t * 64 + 36], h2T[:, k, t * P:(t + 1) * P], wr[:, k, :],
                          start=(k == 0), stop=(k == KB - 1))
        last.then_inc(logits_done, 1)
        pe.wait_ge(hot_ready, 1)
        pe.wait_ge(rconst_ready, 1)
        mm(bank[5][:, 0:E], upper[:, :], em[:, 0, :], start=True, stop=True)
        mm(bank[5][:, E:2 * E], ones[:, :], em[:, 0, :], start=True, stop=False)
        mm(bank[5][:, E:2 * E], upper[:, :], em[:, 1, :], start=False, stop=True)
        mm(bank[5][:, 2 * E:3 * E], ones[:, :], em[:, 0, :], start=True, stop=False)
        mm(bank[5][:, 2 * E:3 * E], ones[:, :], em[:, 1, :], start=False, stop=True).then_inc(rank_done, 1)

        def gather(r1, first=False):
            pe.wait_ge(picked, r1 + 1)
            if not first:
                pe.wait_ge(got_evac, r1 * 4)
            for t in range(TT):
                last = mm(bank[7][:, 0:36], pick[:, t, :, :].rearrange("p e s -> p (e s)"), wtok[:, t, :],
                          start=(t == 0), stop=(t == TT - 1))
            last.then_inc(slots_done, 1)
            for g in range(4):
                if g == 0:
                    pe.wait_ge(slots_evac, r1 + 1)
                else:
                    pe.wait_ge(got_evac, r1 * 4 + g)
                for kk in range(4):
                    for t in range(TT):
                        last = mm(bank[7][:, kk * P:(kk + 1) * P], h[:, t, 4 * g + kk, :],
                                  pick[:, t, :, :].rearrange("p e s -> p (e s)"), start=(t == 0), stop=(t == TT - 1))
                last.then_inc(got_done, 1)

        pe.wait_ge(tables_ready, 1)
        gather(0, first=True)

        def uses(s, i3, more):
            return i3 * 48 + 16 * (FRONT_USES[s] + more)

        def gate_up(slots, o, got):
            for hf in range(2):
                for s in slots[2 * hf:2 * hf + 2]:
                    pe.wait_ge(loaded[s[0]], s[1])
                s = slots[2 * hf][0]
                both = ring[:, s:s + 2, :].rearrange("p m (k n) -> p m k n", k=8)
                for kk in range(8):
                    k = hf * 8 + kk
                    for g in range(2):
                        last = mm(o[CAP * g:CAP * g + CAP, :].rearrange("p (m n) -> p m n", m=2), got(k),
                                  both[:, :, kk, g * T:(g + 1) * T], start=(k == 0), stop=(k == KB - 1))
                yield last

        def pair(r, i, x2):
            for e in range(2):
                pe.wait_ge(act_ready, r * 2 + (e + 1))
                if e == 0:
                    pe.wait_ge(got_evac, r * 4 + 4)
                sl = [(e_chunk(12 * x2 + 4 * e + q)[0],
                       uses(e_chunk(12 * x2 + 4 * e + q)[0], i, e_chunk(12 * x2 + 4 * e + q)[1])) for q in range(4)]
                for last in gate_up(sl, bank[e], lambda k: xeT[:, k, CAP * e:CAP * e + CAP]):
                    last.then_inc(gu_half, 1)
            gather(r + 1)
            for e in range(2):
                pe.wait_ge(act_ready, r * 2 + (e + 3))
                if e == 0:
                    pe.wait_ge(aT_evac, r + 1)
                for cb in range(2):
                    last = tr(bank[2][:, (2 * e + cb) * P:(2 * e + cb + 1) * P], act[:, e, cb * P:(cb + 1) * P],
                              ident[:, :])
            last.then_inc(aT_done, 1)
            pe.wait_ge(aT_evac, r + 2)
            down = []
            for e in range(2):
                for hf in range(2):
                    s, m = e_chunk(12 * x2 + 8 + 2 * e + hf)
                    pe.wait_ge(loaded[s], uses(s, i, m))
                    down.append(s)

            def combine(nb):
                if nb == 0:
                    pe.wait_ge(send_ready, r + 1)
                pe.wait_ge(y_evac, r * 4 + (nb + 3))
                for t in range(TT):
                    pe.wait_ge(comb_added, r * 8 + (nb * 2 + t + 1))
                    mm(bank[5 + t][:, :], send[:, t * P:(t + 1) * P], ye[:, nb * NB:(nb + 1) * NB],
                       start=True, stop=True).then_inc(comb_done, 1)

            for nb in range(DB):
                pe.wait_ge(y_evac, r * 4 + nb + 1)
                for g in range(2):
                    for cb in range(2):
                        for e in range(2):
                            last = mm(bank[3 + nb % 2][CAP * e:CAP * e + CAP, :],
                                      actT[:, e, cb, CAP * g:CAP * g + CAP],
                                      ring[:, down[2 * e + g], cb * D + nb * NB:cb * D + (nb + 1) * NB],
                                      start=(g == 0 and cb == 0), stop=(g == 1 and cb == 1))
                last.then_inc(y_done, 1)
                if nb > 0:
                    combine(nb - 1)
            combine(DB - 1)

        with pe.Fori(0, E // 4) as i:
            for x2 in range(2):
                pair(i * 2 + x2, i, x2)

        pe.wait_ge(tables_ready, 2)
        n_over = pe.value_load(whole[0:1, 8:9], min_val=0, max_val=MAX_OVER)
        with pe.If(n_over > 0):
            pe.wait_ge(got_evac, 4 * (E // 2 + 1))
            with pe.Fori(0, n_over) as j:
                pe.wait_ge(ov_pick, j + 1)
                for t in range(TT):
                    mm(bank[7][0:CAP, 0:2], pick[:, t, 0, :], tover[:, t, :], start=(t == 0), stop=(t == TT - 1))
                for k in range(KB):
                    for t in range(TT):
                        last = mm(bank[5 + k // 8][:, (k % 8) * CAP:(k % 8 + 1) * CAP], h[:, t, k, :],
                                  pick[:, t, 0, :], start=(t == 0), stop=(t == TT - 1))
                last.then_inc(ov_got, 1)
                pe.wait_ge(ov_in, j + 1)
                over_uses = lambda q: j * 16 + 16 * (FRONT_USES[ORDER[q]] + 25)
                sl = [(ORDER[q], over_uses(q)) for q in range(4)]
                for last in gate_up(sl, bank[0], lambda k: xeT[:, k, 0:CAP]):
                    pass
                last.then_inc(ov_gu, 1)
                pe.wait_ge(ov_act, j + 1)
                for cb in range(2):
                    last = tr(bank[2][:, cb * P:(cb + 1) * P], act[:, 0, cb * P:(cb + 1) * P], ident[:, :])
                last.then_inc(ov_aT, 1)
                pe.wait_ge(ov_aTe, j + 1)
                for q in (4, 5):
                    pe.wait_ge(loaded[ORDER[q]], over_uses(q))
                for nb in range(DB):
                    for g in range(2):
                        for cb in range(2):
                            last = mm(bank[3 + nb][0:CAP, :], actT[:, 0, cb, CAP * g:CAP * g + CAP],
                                      ring[:, ORDER[4 + g], cb * D + nb * NB:cb * D + (nb + 1) * NB],
                                      start=(g == 0 and cb == 0), stop=(g == 1 and cb == 1))
                last.then_inc(ov_y, 1)
                pe.wait_ge(ov_ye, j + 1)
                for nb in range(DB):
                    for t in range(TT):
                        last = mm(bank[2 * nb + t][:, :], send[0:CAP, t * P:(t + 1) * P],
                                  ye[0:CAP, nb * NB:(nb + 1) * NB], start=True, stop=True)
                last.then_inc(ov_comb, 1)

    @block.vector
    def _(dve):
        v = nc.vector

        def inverse(n):
            dve.wait_ge(ssq_done, n + 1)
            v.tensor_scalar(inv[:, n, :], ssq[:, n, :], 1.0 / D, EPS, ALU.mult, ALU.add)
            dve.drain()
            v.reciprocal(inv[:, n, :], inv[:, n, :]).then_inc(inv_ready, 1)
            dve.wait_ge(rstd_ready, n + 1)

        dve.sem_inc(biased, 1)
        dve.sem_inc(o_scaled, 1)
        dve.sem_inc(act_ready, 2)
        dve.sem_inc(comb_added, 2)
        dve.wait_ge(const_ready, 1)
        v.tensor_reduce(sel[:, :], ident[:, 0:97:32], AX.X, ALU.add)
        dve.wait_ge(c_sig, 1)
        v.tensor_tensor(cc[:, 2, :], cc[:, 0, :], cc[:, 1, :], ALU.mult)
        dve.drain()
        v.tensor_copy(condb[:, :, :], cc[:, 2, :].unsqueeze(2).broadcast_to([P, KB, 32])).then_inc(cond_ready, 1)
        dve.wait_ge(rows_T, 1)
        v.tensor_copy(badac_flat[:, :], bank[7][:, 0:6 * KB])
        v.tensor_copy(gains_flat[:, :], bank[7][:, P:P + 4 * KB])
        inverse(0)
        for t in range(TT):
            v.tensor_scalar(xn[:, t, :, :], xres[:, t, :].rearrange("p (k q) -> p k q", k=KB),
                            rstd[:, 0, t:t + 1], None, ALU.mult).then_inc(xn_ready, 1)
        for g in range(8):
            t, kq = g // 4, g % 4
            dve.wait_ge(xT_done, g + 1)
            v.tensor_copy(xnT[:, 4 * kq:4 * kq + 4, t * P:(t + 1) * P],
                          bank[5 + g % 2][:, :].rearrange("p (k q) -> p k q", k=4)).then_inc(xT_evac, 1)

        def split_steps(s, count, u, k0=0, k1=8):
            if k0 == 0:
                dve.wait_ge(loaded[s], count)
            hi_of = lambda k: w_hi[:, k % SPLITS, :]
            for k in range(k0, k1 + 1):
                if k < k1:
                    dve.wait_ge(split_used, u + (k + 1))
                    v.tensor_copy(hi_of(k), ring[:, s, k * NB:(k + 1) * NB]).then_inc(hi_done, 1)
                if k > k0:
                    dve.wait_ge(hi_done, u + k)
                    v.tensor_tensor(w_lo[:, (k - 1) % SPLITS, :], ring[:, s, (k - 1) * NB:k * NB],
                                    hi_of(k - 1).bitcast(F32), ALU.subtract).then_inc(split_ready, 1)

        for q in range(QUARTERS):
            cut = slice(4 * q, 4 * q + 4)
            dve.wait_ge(col_evac, 2 * q + 3)
            v.tensor_tensor(msum[:, 0:2, cut], msum[:, 0:2, cut], badac[:, 0:2, cut], ALU.add)
            dve.drain()
            v.scalar_tensor_tensor(colA[:, cut], msum[:, 1, cut], 1.0, gains[:, 0, cut], ALU.add, ALU.mult)\
                .then_inc(colA_ready, 1)
            dve.wait_ge(xnT_mod, 4 * (q + 1))
            v.tensor_copy(hT_hi[:, cut, :], xnT[:, cut, :])
            dve.drain()
            v.tensor_tensor(hT_lo[:, cut, :], xnT[:, cut, :], hT_hi[:, cut, :].bitcast(F32), ALU.subtract)\
                .then_inc(hT_ready, 1)
            split_steps(*front(5 * q + 4), 8 * q)
        with dve.Fori(0, 6) as b:
            for q in range(2):
                split_steps(2 + q, b * 16 + 16 * (C_BLOCKS // 4 + 1), b * KB + (U_BLOCKS + 8 * q))
        for q in range(2):
            split_steps(*front(C_KV + 2 + q), U_BLOCKS + 6 * KB + 8 * q)
        dve.wait_ge(sink_loaded, 16)
        v.tensor_scalar(nsink[:, :], sink[:, :], -1.0, None, ALU.mult)
        dve.drain()

        SB = (3, 4)
        dve.wait_ge(const_ready, 1)

        def bias_max(R, r, i):
            b = r % 2
            dve.wait_ge(scored, R + 3)
            dve.wait_ge(pt_done, R * 2)
            for hh in range(2):
                head = i * 4 + ((r // 2) * 2 + hh)
                last = v.scalar_tensor_tensor(sc[:, b, hh, :], dist[:, b:b + 3, :].rearrange("p a k -> p (a k)"),
                                              nslope[:, bass.ds(head, 1)], bank[SB[hh]][:, 0:3 * P],
                                              ALU.mult, ALU.add)
            last.then_inc(biased, 1)
            dve.drain()
            t1, t0 = (slice(0, 256), slice(256, 384)) if b == 0 else (slice(128, 384), slice(0, 128))
            for t, cut in ((0, t0), (1, t1)):
                v.tensor_reduce(mx[:, b, :, t], sc[:, b, :, cut], AX.X, ALU.max)
            dve.drain()
            if b == 0:
                v.tensor_scalar(nm[:, b, :, :], mx[:, b, :, :], -0.125, None, ALU.mult).then_inc(nm_ready, 1)
            else:
                v.tensor_scalar(nm[:, b, :, :], mx[:, b, :, :], -0.125, None, ALU.mult)
                dve.drain()
                head = i * 4 + (r // 2) * 2
                v.tensor_tensor(nm[:, b, :, :], nm[:, b, :, :],
                                nsink[:, bass.ds(head, 2)].unsqueeze(2).broadcast_to([P, 2, TT]), ALU.min)\
                    .then_inc(nm_ready, 1)

        def o_scale(R, r):
            b = r % 2
            dve.wait_ge(exped, R + 1)
            if b == 1:
                v.tensor_tensor(den[:, b, :, :], den[:, b, :, :], esink[:, b, :, :], ALU.add)
                dve.drain()
            v.reciprocal(den[:, b, :, :], den[:, b, :, :])
            dve.drain()
            dve.wait_ge(pv_done, R * 2 + 3)
            dve.wait_ge(ot_done, R + 1)
            for hh in range(2):
                last = v.tensor_tensor(osb[:, :, hh, :],
                                       bank[6][:, hh * P:(hh + 1) * P].rearrange("p (t d) -> p t d", t=TT),
                                       den[:, b, hh, :].unsqueeze(2).broadcast_to([P, TT, HD]), ALU.mult)
            last.then_inc(o_scaled, 1)

        bias_max(0, 0, 0)
        with dve.Fori(0, 4) as i:
            for r in range(4):
                at = (r % 2, i * 32 + 16 * (r // 2 + 1 + (C_GATES + 2) // 4), i * 32 + (U_GATES + 8 * r))
                split_steps(*at, 0, 7)
                bias_max(i * 4 + (r + 1), r + 1, i)
                o_scale(i * 4 + r, r)
                split_steps(*at, 7, 8)
        dve.wait_ge(col_evac, ADA_BLOCKS + 1)
        v.tensor_tensor(msum[:, 2:6, :], msum[:, 2:6, :], badac[:, 2:6, :], ALU.add)
        dve.drain()
        for n, m, g in ((0, 2, 1), (3, 5, 3)):
            v.tensor_tensor(vecs[:, n, :], msum[:, m, :], gains[:, g, :], ALU.mult)
        v.tensor_copy(vecs[:, 1, :], msum[:, 3, :])
        v.scalar_tensor_tensor(vecs[:, 2, :], msum[:, 4, :], 1.0, gains[:, 2, :], ALU.add, ALU.mult)
        dve.drain().then_inc(vecs_ready, 1)

        dve.wait_ge(ot_evac, 17)
        dve.wait_ge(split_used, U_IN_END + CREDIT)
        for m in range(2):
            src = qk[:, 16 * m:16 * m + 8, :]
            cut = slice(8 * m, 8 * m + 8)
            v.tensor_copy(hT_hi[:, cut, :], src)
            dve.drain()
            v.tensor_tensor(hT_lo[:, cut, :], src, hT_hi[:, cut, :].bitcast(F32), ALU.subtract).then_inc(oT_split, 1)

        def gate_out(nb):
            dve.wait_ge(gate_ready, nb + 1)
            dve.wait_ge(split_used, U_IN_END + 16 * (nb + 1) + CREDIT)
            for m, gt in ((0, gateA), (1, gateB)):
                for t in range(TT):
                    cut = gt[:, t, nb * NB:(nb + 1) * NB]
                    last = v.tensor_tensor(cut, cut, bank[4 * (nb % 2) + 2 * m + t][:, :], ALU.mult)
            last.then_inc(gated, 1)

        for n in range(8):
            split_steps(*front(C_O + n), U_IN_END + 8 * n, 0, 4)
            if n % 2 == 0 and n > 0:
                gate_out(n // 2 - 1)
            split_steps(*front(C_O + n), U_IN_END + 8 * n, 4, 8)
        gate_out(DB - 1)
        for g in range(8):
            t, kq = g // 4, g % 4
            dve.wait_ge(yT_hi, g + 1)
            cut = (slice(None), slice(4 * kq, 4 * kq + 4), slice(t * P, (t + 1) * P))
            v.tensor_tensor(hT_lo[cut], bank[g % 4][:, :].rearrange("p (k q) -> p k q", k=4),
                            hT_hi[cut].bitcast(F32), ALU.subtract).then_inc(yT_ready, 1)
        for n in range(8, 16):
            split_steps(*front(C_O + n), U_IN_END + 8 * n)

        dve.wait_ge(rowm_loaded, 48)
        dve.wait_ge(x_again, 16)
        inverse(1)
        for t in range(TT):
            v.scalar_tensor_tensor(y2[:, t, :], y2[:, t, :], rstd[:, 1, t:t + 1], rowGm[:, :], ALU.mult, ALU.mult)
        dve.drain()
        v.tensor_tensor(xres[:, :, :], xres[:, :, :], y2[:, :, :], ALU.add)
        dve.drain().then_inc(x2_ready, 1)
        by_block = lambda ap: ap.rearrange("p (q k) -> p k q", k=KB)
        inverse(2)
        for t in range(TT):
            v.scalar_tensor_tensor(h[:, t, :, :], by_block(xres[:, t, :]), rstd[:, 2, t:t + 1],
                                   by_block(rowAf[:, :]), ALU.mult, ALU.mult)
        dve.drain()
        for t in range(TT):
            v.tensor_tensor(h[:, t, :, :], h[:, t, :, :], by_block(rowSf[:, :]), ALU.add).then_inc(h_ready, 1)

        def wide(ap, n):
            return ap.unsqueeze(2).broadcast_to([P, TT, n])

        def first_of(hot, vals, top, order, tmp, n):
            v.tensor_tensor(tmp, vals, wide(top, n), ALU.is_equal)
            dve.drain()
            v.tensor_tensor(tmp, tmp, order.unsqueeze(1).broadcast_to([P, TT, n]), ALU.mult)
            dve.drain()
            v.tensor_reduce(m3[:, 3, :], tmp, AX.X, ALU.max)
            dve.drain()
            v.tensor_tensor(hot, tmp, wide(m3[:, 3, :], n), ALU.is_equal)
            dve.drain()

        dve.wait_ge(rconst_ready, 1)
        dve.wait_ge(logits_done, 1)
        v.tensor_tensor(lg[:, :, :], bank[4][:, 0:P].rearrange("p (t n) -> p t n", t=TT)[:, :, 0:36],
                        rbias[:, :].unsqueeze(1).broadcast_to([P, TT, 36]), ALU.add)
        dve.drain()
        v.tensor_reduce(m3[:, 0, :], lg[:, :, 0:GROUPS], AX.X, ALU.max)
        dve.drain()
        v.tensor_tensor(ex[:, :, 0:GROUPS], lg[:, :, 0:GROUPS], wide(m3[:, 0, :], GROUPS), ALU.subtract)
        first_of(goh[:, :, :], lg[:, :, 0:GROUPS], m3[:, 0, :], desc[:, 0:GROUPS], tg[:, :, :], GROUPS)
        v.tensor_scalar(tg[:, :, :], goh[:, :, :], -1.0, 1e30, ALU.add, ALU.mult)
        dve.drain()
        for t in range(TT):
            v.tensor_tensor(em[:, t, :].rearrange("p (g e) -> p g e", g=GROUPS),
                            lg[:, t, GROUPS:36].rearrange("p (g e) -> p g e", g=GROUPS),
                            tg[:, t, :].unsqueeze(2).broadcast_to([P, GROUPS, PER_GROUP]), ALU.add)
        dve.drain()
        v.tensor_reduce(m3[:, 1, :], em[:, :, :], AX.X, ALU.max)
        dve.drain()
        first_of(oh1[:, :, :], em[:, :, :], m3[:, 1, :], desc[:, :], te[:, :, :], E)
        v.scalar_tensor_tensor(em[:, :, :], oh1[:, :, :], -3e30, em[:, :, :], ALU.mult, ALU.add)
        dve.drain()
        v.tensor_reduce(m3[:, 2, :], em[:, :, :], AX.X, ALU.max)
        dve.drain()
        v.tensor_tensor(ex[:, :, 4], m3[:, 2, :], m3[:, 1, :], ALU.subtract)
        dve.drain().then_inc(ex_in, 1)
        first_of(oh2[:, :, :], em[:, :, :], m3[:, 2, :], desc[:, :], te[:, :, :], E)
        v.tensor_tensor(em[:, :, :], oh1[:, :, :], oh2[:, :, :], ALU.add)
        dve.drain().then_inc(hot_ready, 1)
        dve.wait_ge(ex_done, 1)
        v.tensor_reduce(m3[:, 0, :], ex[:, :, 0:GROUPS], AX.X, ALU.add)
        dve.drain()
        v.scalar_tensor_tensor(m3[:, 0, :], ex[:, :, 4], 1.0, m3[:, 0, :], ALU.add, ALU.mult)
        dve.drain()
        v.reciprocal(m3[:, 1, :], m3[:, 0, :])
        dve.drain()
        v.tensor_tensor(m3[:, 2, :], m3[:, 1, :], ex[:, :, 4], ALU.mult)
        v.tensor_tensor(oh1[:, :, :], oh1[:, :, :], wide(m3[:, 1, :], E), ALU.mult)
        dve.drain()
        v.tensor_tensor(oh2[:, :, :], oh2[:, :, :], wide(m3[:, 2, :], E), ALU.mult)
        dve.drain()
        v.tensor_tensor(wtok[:, :, 0:E], oh1[:, :, :], oh2[:, :, :], ALU.add)
        dve.wait_ge(rank_done, 1)
        v.scalar_tensor_tensor(te[:, :, :], bank[5][:, 0:2 * E].rearrange("p (t e) -> p t e", t=TT), 1.0,
                               em[:, :, :], ALU.add, ALU.mult)
        dve.drain()
        v.tensor_scalar(rank[:, :, 0:E], te[:, :, :], -1.0, None, ALU.add)
        dve.drain().then_inc(tables_ready, 1)

        def pick_pair(r1, first=False):
            if not first:
                dve.wait_ge(got_done, r1 * 4)
            for t in range(TT):
                last = v.tensor_tensor(pick[:, t, :, :],
                                       iota[:, 0:CAP].unsqueeze(1).broadcast_to([P, 2, CAP]),
                                       rank[:, t, bass.ds(r1 * 2, 2)].unsqueeze(2).broadcast_to([P, 2, CAP]),
                                       ALU.is_equal)
            last.then_inc(picked, 1)

        pick_pair(0, first=True)
        v.tensor_scalar(cnt[:, :], bank[5][:, 2 * E:3 * E], float(CAP), None, ALU.is_gt)
        for n in (2, 3):
            v.tensor_scalar(te[:, n - 2, :], bank[5][:, 2 * E:3 * E], float(CAP * n), None, ALU.is_gt)
        dve.drain()
        for n in (0, 1):
            v.tensor_tensor(cnt[:, :], cnt[:, :], te[:, n, :], ALU.add)
            dve.drain()
        v.tensor_tensor_scan(cum[:, :], ones[:, 0:E], cnt[:, :], 0.0, ALU.mult, ALU.add)
        dve.drain()
        v.tensor_tensor(cmpj[:, :, :], cum[:, :].unsqueeze(1).broadcast_to([P, 8, E]),
                        iota[:, 0:8].unsqueeze(2).broadcast_to([P, 8, E]), ALU.is_le)
        v.tensor_tensor(cnt[:, :], cum[:, :], cnt[:, :], ALU.subtract)
        v.tensor_scalar(te[:, :, :], rank[:, :, 0:E], CAP - 0.5, None, ALU.is_gt)
        v.tensor_copy(whole[:, 8:9], cum[:, E - 1:E])
        dve.drain()
        v.tensor_reduce(eidf[:, :], cmpj[:, :, :], AX.X, ALU.add)
        v.tensor_scalar(cnt[:, :], cnt[:, :], float(CAP), 1.0 - CAP, ALU.mult, ALU.add)
        dve.drain()
        v.tensor_scalar(whole[:, 0:8], eidf[:, :], float(E - 1), None, ALU.min)
        v.tensor_tensor(over[:, :, :], rank[:, :, 0:E], cnt[:, :].unsqueeze(1).broadcast_to([P, TT, E]), ALU.add)
        dve.drain()
        v.tensor_tensor(over[:, :, :], over[:, :, :], te[:, :, :], ALU.mult)
        dve.drain()
        v.tensor_scalar(over[:, :, :], over[:, :, :], -1.0, None, ALU.add)
        dve.drain().then_inc(tables_ready, 1)

        def send_matrix(rows, weight_col):
            return v.tensor_scalar(send[0:rows, :], iota[0:rows, :], slot[0:rows, weight_col[0]:weight_col[0] + 1],
                                   weight_col[1], ALU.is_equal, ALU.mult)

        def pair(r):
            dve.wait_ge(slots_evac, r + 1)
            for e in range(2):
                v.tensor_copy(wsel[CAP * e:CAP * e + CAP, 0:1], slot[CAP * e:CAP * e + CAP, bass.ds(r * 2 + e, 1)])
                v.tensor_copy(wsel[CAP * e:CAP * e + CAP, 1:2], slot[CAP * e:CAP * e + CAP, 34:35])
            dve.drain()
            pick_pair(r + 1)
            dve.wait_ge(comb_done, r * 8 + 8)
            v.tensor_scalar(send[:, :], iota[:, :], wsel[:, 1:2], wsel[:, 0:1], ALU.is_equal, ALU.mult)\
                .then_inc(send_ready, 1)
            for e in range(2):
                dve.wait_ge(sig_done, r * 2 + (e + 1))
                v.tensor_tensor(act[:, e, :], act[:, e, :], bank[e][:, 0:T], ALU.mult)
                dve.drain()
                v.tensor_tensor(act[:, e, :], act[:, e, :], bank[e][:, T:2 * T], ALU.mult).then_inc(act_ready, 1)
            for nb in range(DB):
                for t in range(TT):
                    dve.wait_ge(comb_done, r * 8 + (nb * 2 + t + 9))
                    cut = acc[:, t, nb * NB:(nb + 1) * NB]
                    v.tensor_tensor(cut, cut, bank[5 + t][:, :], ALU.add).then_inc(comb_added, 1)

        dve.wait_ge(acc_zero, 1)
        with dve.Fori(0, E // 4) as i:
            for x2 in range(2):
                pair(i * 2 + x2)

        dve.wait_ge(comb_added, 4 * E + 2)
        dve.sem_inc(ov_go, 1)
        n_over = dve.value_load(whole[0:1, 8:9], min_val=0, max_val=MAX_OVER)
        with dve.If(n_over > 0):
            dve.wait_ge(got_done, 4 * (E // 2 + 1))
            with dve.Fori(0, n_over) as j:
                v.tensor_scalar(te[:, :, :], over[:, :, :], -0.5, None, ALU.is_gt)
                v.tensor_scalar(oh1[:, :, :], over[:, :, :], CAP - 0.5, None, ALU.is_lt)
                dve.drain()
                v.tensor_tensor(te[:, :, :], te[:, :, :], oh1[:, :, :], ALU.mult)
                dve.drain()
                v.scalar_tensor_tensor(oh1[:, :, :], over[:, :, :], 1.0, te[:, :, :], ALU.add, ALU.mult)
                v.tensor_tensor(oh2[:, :, :], wtok[:, :, 0:E], te[:, :, :], ALU.mult)
                dve.drain()
                v.tensor_reduce(rover[:, :], oh1[:, :, :], AX.X, ALU.add)
                v.tensor_reduce(tover[:, :, 0], oh2[:, :, :], AX.X, ALU.add)
                v.tensor_copy(tover[:, :, 1], wtok[:, :, 34])
                v.tensor_scalar(over[:, :, :], over[:, :, :], -float(CAP), None, ALU.add)
                dve.drain()
                v.tensor_scalar(rover[:, :], rover[:, :], -1.0, None, ALU.add)
                dve.drain()
                for t in range(TT):
                    last = v.tensor_scalar(pick[:, t, 0, :], iota[:, 0:CAP], rover[:, t:t + 1], None, ALU.is_equal)
                last.then_inc(ov_pick, 1)
                dve.wait_ge(ov_in, j + 1)
                v.tensor_scalar(send[0:CAP, :], iota[0:CAP, :], slot[0:CAP, 1:2], slot[0:CAP, 0:1],
                                ALU.is_equal, ALU.mult)
                dve.wait_ge(ov_sig, j + 1)
                v.tensor_tensor(act[:, 0, :], act[:, 0, :], bank[0][:, 0:T], ALU.mult)
                dve.drain()
                v.tensor_tensor(act[:, 0, :], act[:, 0, :], bank[0][:, T:2 * T], ALU.mult).then_inc(ov_act, 1)
                dve.wait_ge(ov_comb, j + 1)
                for nb in range(DB):
                    for t in range(TT):
                        cut = acc[:, t, nb * NB:(nb + 1) * NB]
                        last = v.tensor_tensor(cut, cut, bank[2 * nb + t][:, :], ALU.add)
                last.then_inc(ov_go, 1)
        dve.drain().then_inc(acc_final, 1)
        inverse(3)
        dve.wait_ge(rowf_loaded, 16)
        for t in range(TT):
            v.scalar_tensor_tensor(acc[:, t, :], acc[:, t, :], rstd[:, 3, t:t + 1], rowGf[:, :], ALU.mult, ALU.mult)
            dve.drain()
            v.tensor_tensor(xres[:, t, :], xres[:, t, :], acc[:, t, :], ALU.add).then_inc(fin_ready, 1)

    block.__exit__(None, None, None)


_INS = ["x", "c", "w_ada", "b_ada", "g_pre_mix", "g_post_mix", "w_in", "swa_sinks", "w_o_moba", "w_o_swa", "w_out",
        "g_pre_ffn", "g_post_ffn", "w_router_group", "b_router_group", "w_router_expert", "b_router_expert",
        "w_gate", "w_up", "w_down"]


def kernel(**inputs):
    import numpy as np
    import concourse.bacc as bacc
    from concourse import mybir as _mybir
    from concourse.bass_utils import run_bass_kernel_spmd

    nc = bacc.Bacc("TRN2", target_bir_lowering=False, num_devices=1)
    arrays, args = {}, []
    for name in _INS:
        a = np.ascontiguousarray(inputs[name])
        arrays[f"in_{name}"] = a
        args.append(nc.dram_tensor(f"in_{name}", a.shape, _mybir.dt.from_np(a.dtype), kind="ExternalInput").ap())
    out = nc.dram_tensor("out_0", (1, T, D), F32, kind="ExternalOutput").ap()
    decoder_block(nc, *args, out)
    r = run_bass_kernel_spmd(nc, [arrays], core_ids=[0])
    return r.results[0]["out_0"]
```

```python
import concourse.bass as bass
from concourse import mybir

F32 = mybir.dt.float32
F32R = mybir.dt.float32r
I32 = mybir.dt.int32
ALU = mybir.AluOpType
ACT = mybir.ActivationFunctionType
AX = mybir.AxisListType

P = 128
D = 2048
T = 256
TT = T // P
KB = D // P
NB = 512
DB = D // NB
IN_COLS = 8704
HD = 64
HEADS = 16
PAIRS = HEADS // 2
KV = 4
GROUPS, PER_GROUP = 4, 8
E = GROUPS * PER_GROUP
FE = 512
CAP = 64
EPS = 1e-6
MASKED = 1e30
ADA_BLOCKS = 6 * D // NB
QUARTERS = 4
ADA_FIRST = 2 * QUARTERS
SPLITS = 4
SLOT = 8 * NB
MAX_OVER = TT * P * 2 // (CAP + 1) + 1

COL_QA, COL_KA, COL_VA, COL_QB, COL_KVB, COL_G = 0, 1024, 2048, 3072, 4096, 4608


def decoder_block(nc, x, c, w_ada, b_ada, g_pre_mix, g_post_mix, w_in, swa_sinks, w_o_moba, w_o_swa, w_out,
                  g_pre_ffn, g_post_ffn, w_router_group, b_router_group, w_router_expert, b_router_expert,
                  w_gate, w_up, w_down, out):
    base = 16512

    def place(name, shape, dtype, at):
        return nc.alloc_sbuf_tensor_at(name, shape, dtype, offset=base + at)

    RING, V, XRES, SM = 0, 131072, 186368, 202752
    ring = place("ring", [P, 8, SLOT], F32, RING)
    xres = place("xres", [P, TT, D], F32, XRES)
    U0 = 65536
    hT_hi = place("hT_hi", [P, KB, T], F32R, U0)
    hT_lo = place("hT_lo", [P, KB, T], F32R, U0 + 16384)
    w_hi = place("w_hi", [P, SPLITS, NB], F32R, U0 + 32768)
    w_lo = place("w_lo", [P, SPLITS, NB], F32R, U0 + 40960)
    gates = place("gates", [P, TT, 2 * D], F32, U0 + 49152)
    gateA, gateB = gates[:, :, 0:D], gates[:, :, D:2 * D]
    xn = place("xn", [P, TT, KB, P], F32, U0 + 49152)
    qz = place("qz", [P, 2, 2, T], F32, XRES)
    sc = place("sc", [P, 2, 2, 3 * P], F32, XRES + 4096)
    pT = place("pT", [P, 2, 3 * P], F32, XRES + 10240)
    osb = place("osb", [P, TT, 2, HD], F32, XRES + 13312)
    mx = place("mx", [P, 2, 2, TT], F32, XRES + 14336)
    nm = place("nm", [P, 2, 2, TT], F32, XRES + 14368)
    den = place("den", [P, 2, 2, TT], F32, XRES + 14400)
    esink = place("esink", [P, 2, 2, TT], F32, XRES + 14432)
    qk = place("qk", [P, 24, T], F32, V + 16384)
    vA = place("vA", [P, TT, HEADS * HD], F32, V + 40960)
    kB = place("kB", [P, KV, T], F32, V + 49152)
    vB = place("vB", [P, TT, KV * HD], F32, V + 53248)
    xnT = place("xnT", [P, KB, T], F32, V)
    oA_hi = place("oA_hi", [P, 8, T], F32R, V + 24576)
    oA_lo = place("oA_lo", [P, 8, T], F32R, V + 40960)
    wo_hi = place("wo_hi", [P, SPLITS, NB], F32R, V + 32768)
    wo_lo = place("wo_lo", [P, SPLITS, NB], F32R, V + 40960)
    y2 = place("y2", [P, TT, D], F32, V + 16384)
    h = place("h", [P, TT, KB, P], F32, V + 16384)
    acc = place("acc", [P, TT, D], F32, V)
    rowGm = place("rowGm", [P, D], F32, V)
    dump_y = place("dump_y", [P, D], F32, V + 8192)
    x2T = place("x2T", [P, KB, T], F32, V + 32768)
    xeT = place("xeT", [P, KB, P], F32, V + 32768)
    rowGf = place("rowGf", [P, D], F32, 6 * 16384)
    dump_a = place("dump_a", [P, NB], F32, 6 * 16384 + 8192)
    acc_g = place("acc_g", [P, TT, D], F32, 7 * 16384)
    ye = place("ye", [P, D], F32, V + 40960)
    pick = place("pick", [P, TT, 2, CAP], F32, V + 49152)
    send = place("send", [P, T], F32, V + 50176)
    act = place("act", [P, 2, T], F32, V + 51200)
    logT = place("logT", [P, T], F32, V + 53248)
    fold = place("fold", [P, 36], F32, V + 54272)
    actT = place("actT", [P, 2, 2, P], F32, V + 53248)
    mb = place("mb", [P, NB], F32, SM)
    condb = place("condb", [P, KB, 32], F32, SM + 2048)
    dist = place("dist", [P, 4, P], F32, SM + 4096)
    brow = place("brow", [6 * KB, P], F32, SM + 6144)
    grow = place("grow", [4 * KB, P], F32, SM + 6656)
    vrow = place("vrow", [4 * KB, P], F32, SM + 7168)
    ident = place("ident", [P, P], F32, SM + 7680)
    msum_flat = place("msum", [P, 6 * KB], F32, SM + 8192)
    msum = msum_flat[:, :].rearrange("p (v k) -> p v k", k=KB)
    badac_flat = place("badac", [P, 6 * KB], F32, SM + 8576)
    badac = badac_flat[:, :].rearrange("p (v k) -> p v k", k=KB)
    gains_flat = place("gains", [P, 4 * KB], F32, SM + 8960)
    gains = gains_flat[:, :].rearrange("p (v k) -> p v k", k=KB)
    vecs = place("vecs", [P, 4, KB], F32, SM + 9216)
    colA = place("colA", [P, KB], F32, SM + 9472)
    cc = place("cc", [P, 3, KB], F32, SM + 9536)
    gainF = place("gainF", [P, KB], F32, SM + 9472)
    shiftF = place("shiftF", [P, KB], F32, SM + 9536)
    ssq_part = place("ssq_part", [P, TT, DB], F32, SM + 5856)
    ssq = place("ssq", [P, 4, TT], F32, SM + 9728)
    inv = place("inv", [P, 4, TT], F32, SM + 9760)
    rstd = place("rstd", [P, 4, TT], F32, SM + 9792)
    nslope = place("nslope", [P, HEADS + 2], F32, SM + 9824)
    sink = place("sink", [P, HEADS], F32, SM + 9920)
    sel = place("sel", [P, 1], F32, SM + 10048)
    nsink = place("nsink", [P, HEADS], F32, SM + 9984)
    iota = place("iota", [P, T], F32, SM)
    wtok = place("wtok", [P, TT, 36], F32, SM + 1024)
    rank = place("rank", [P, TT, 34], F32, SM + 1312)
    wr = place("wr", [P, KB, 36], F32, SM + 1600)
    rbias = place("rbias", [P, 36], F32, SM + 3904)
    lg = place("lg", [P, TT, 36], F32, SM + 4064)
    em = place("em", [P, TT, E], F32, SM + 4352)
    oh1 = place("oh1", [P, TT, E], F32, SM + 4608)
    oh2 = place("oh2", [P, TT, E], F32, SM + 4864)
    te = place("te", [P, TT, E], F32, SM + 5120)
    tg = place("tg", [P, TT, 4], F32, SM + 5376)
    goh = place("goh", [P, TT, 4], F32, SM + 5408)
    ex = place("ex", [P, TT, 5], F32, SM + 5440)
    m3 = place("m3", [P, 4, TT], F32, SM + 5504)
    slot = place("slot", [P, 36], F32, SM + 5536)
    wsel = place("wsel", [P, 2], F32, SM + 5824)
    desc = place("desc", [P, E], F32, SM + 5696)
    upper = place("upper", [P, P], F32, SM + 6144)
    ones = place("ones", [P, P], F32, SM + 6656)
    over = place("over", [P, TT, E], F32, SM + 7168)
    tover = place("tover", [P, TT, 2], F32, SM + 7424)
    rover = place("rover", [P, TT], F32, SM + 7456)
    swr = place("swr", [P, KB, 36], F32, V + 49152)
    swp = place("swp", [P, 36], F32, SM + 4064)
    cnt = place("cnt", [P, E], F32, SM + 4064)
    cum = place("cum", [P, E], F32, SM + 4192)
    whole = place("whole", [P, 16], I32, SM + 7488)
    cmpj = place("cmpj", [P, 8, E], F32, V + 40960)
    eidf = place("eidf", [P, 8], F32, SM + 7552)

    bank = [nc.alloc_psum_tensor(f"bank{i}", [P, NB], F32) for i in range(8)]

    mod_rows = nc.dram_tensor("mod_rows", [4, D], F32, kind="Internal").ap()

    ada_v = w_ada[0].rearrange("(p h k) n -> p h k n", p=P, h=2)
    in_q = w_in[0].rearrange("(q k p) n -> p q k n", p=P, q=QUARTERS)
    in_v = w_in[0].rearrange("(h k p) n -> p h k n", p=P, h=2)
    out_v = w_out[0].rearrange("(h k p) n -> p h k n", p=P, h=2)
    oA_v = w_o_moba[0].rearrange("(k p) n -> p k n", p=P)
    oB_v = w_o_swa[0].rearrange("(k p) n -> p k n", p=P)
    gate_v = w_gate[0].rearrange("e (p h k) f -> e p h (k f)", p=P, h=2)
    up_v = w_up[0].rearrange("e (p h k) f -> e p h (k f)", p=P, h=2)
    down_v = w_down[0].rearrange("e (h c p) d -> e h p c d", p=P, h=2)
    x_v = x[0].rearrange("(t p) d -> p t d", p=P)
    out_t = out[0].rearrange("(t p) d -> t p d", p=P)

    def sem(name):
        return nc.alloc_semaphore(name)

    loaded = [sem(f"slot{s}_loaded") for s in range(8)]
    x_loaded, sink_loaded, rows_loaded, c_loaded, x_again = map(sem, (
        "x_loaded", "sink_loaded", "rows_loaded", "c_loaded", "x_again"))
    rows_T, cols_ready, vecs_T, vecs_rowed = map(sem, ("rows_T", "cols_ready", "vecs_T", "vecs_rowed"))
    c_sig, cond_ready, const_ready = map(sem, ("c_sig", "cond_ready", "const_ready"))
    ssq_done, inv_ready, rstd_ready = map(sem, ("ssq_done", "inv_ready", "rstd_ready"))
    xn_ready, xT_done, xT_evac = map(sem, ("xn_ready", "xT_done", "xT_evac"))
    ada_half, ada_evac, col_done, col_evac = map(sem, ("ada_half", "ada_evac", "col_done", "col_evac"))
    colA_ready, xnT_mod, hT_ready = map(sem, ("colA_ready", "xnT_mod", "hT_ready"))
    hi_done, split_ready, split_used, block_evac = map(sem, ("hi_done", "split_ready", "split_used", "block_evac"))
    vecs_ready, rows_stored, rowm_loaded, colf_loaded, rowf_loaded = map(sem, (
        "vecs_ready", "rows_stored", "rowm_loaded", "colf_loaded", "rowf_loaded"))
    qz_zero, qz_ready, scored, biased, nm_ready, exped = map(sem, (
        "qz_zero", "qz_ready", "scored", "biased", "nm_ready", "exped"))
    pt_done, pt_evac, pv_done, o_scaled, ot_done, ot_evac = map(sem, (
        "pt_done", "pt_evac", "pv_done", "o_scaled", "ot_done", "ot_evac"))
    gate_ready = sem("gate_ready")
    oT_split, gated, y_added, yT_done, yT_hi, yT_ready = map(sem, (
        "oT_split", "gated", "y_added", "yT_done", "yT_hi", "yT_ready"))
    y2_squared, y2_evac, x2_ready, h_ready, x2T_done, x2T_evac = map(sem, (
        "y2_squared", "y2_evac", "x2_ready", "h_ready", "x2T_done", "x2T_evac"))
    count_done, first_gate, down_half = map(sem, ("count_done", "first_gate", "down_half"))
    x2T_evac1, logT_done, logT_evac = map(sem, ("x2T_evac1", "logT_done", "logT_evac"))
    shift_in, shift_done = map(sem, ("shift_in", "shift_done"))
    router_loaded, rconst_ready, logits_done, ex_in, ex_done, hot_ready, rank_done, tables_ready = map(sem, (
        "router_loaded", "rconst_ready", "logits_done", "ex_in", "ex_done", "hot_ready", "rank_done",
        "tables_ready"))
    acc_zero, picked, slots_done, slots_evac, got_done, got_evac = map(sem, (
        "acc_zero", "picked", "slots_done", "slots_evac", "got_done", "got_evac"))
    gu_half, sig_done, act_ready, aT_done, aT_evac = map(sem, (
        "gu_half", "sig_done", "act_ready", "aT_done", "aT_evac"))
    y_done, y_evac, send_ready, comb_done, comb_added = map(sem, (
        "y_done", "y_evac", "send_ready", "comb_done", "comb_added"))
    ov_go, ov_pick, ov_got, ov_in, ov_gu, ov_sig, ov_act, ov_aT, ov_aTe, ov_y, ov_ye, ov_comb = (
        sem(f"over_{n}") for n in ("go", "pick", "got", "in", "gu", "sig", "act", "aT", "aTe", "y", "ye", "comb"))
    ov_done = sem("over_done")
    piece_loaded = [sem(f"piece{n}_loaded") for n in range(2)]
    fin_ready, stored = sem("fin_ready"), sem("stored")

    OVER_SLOTS = [0, 1, 4, 5, 2, 3]
    DOWN = (3, 4, 0, 1)
    PIECES = ((0, 2), (2, 3), (3, 4))
    LAST = E // 2 - 1
    FRONT_USES = [25, 25, 24, 24, 0, 0, 0, 0]
    ORDER = [6, 7, 2, 3, 0, 1, 4, 5]
    C_BLOCKS, C_KV = 20, 44
    C_GATES, C_O = 50, 82
    U_BLOCKS = 2 * KB
    U_GATES = U_BLOCKS + 7 * KB
    U_IN_END = U_GATES + 8 * KB
    U_O_END = U_IN_END + 2 * DB * 8
    U_END = U_O_END + DB * KB
    CREDIT = SPLITS

    O_BANKS = ((2, 3), (4, 5), (0, 1))
    Y_BANKS = ((0, 1), (2, 3))
    FIRST_GATHER, GATHER = (1, 3, 4, 6), (3, 4, 7, 3)

    def slot4(s):
        return ring[:, s, :].rearrange("p (k n) -> p k n", k=8)

    def e_chunk(m):
        return ORDER[m % 8], m // 8 + 1

    def front(c):
        return c % 4, 16 * (c // 4 + 1)

    block = nc.Block()
    block.__enter__()

    @block.sync
    def _(sp):
        def load(s, src):
            shape4 = len(src.shape) == 3
            dst = slot4(s) if shape4 and src.shape[1] == 8 else (
                ring[:, s, :].rearrange("p (c d) -> p c d", c=2) if shape4 else ring[:, s, :])
            sp.dma_start(dst, src).then_inc(loaded[s], 16)

        def cols(v, hf, at):
            return v[:, hf, :, bass.ds(at, NB)]

        sp.dma_start(xres[:, :, :], x_v).then_inc(x_loaded, 16)
        for n in range(C_BLOCKS):
            q, part = n // 5, n % 5
            if n == 1:
                sp.wait_ge(c_loaded, 16)
            if n >= 4:
                q0, part0 = (n - 4) // 5, (n - 4) % 5
                if part0 < 4:
                    sp.wait_ge(ada_half, 4 * q0 + part0 + 1)
                else:
                    sp.wait_ge(split_ready, 8 * (q0 + 1))
            if part < 4:
                load(n % 4, cols(ada_v, part % 2, (part // 2) * D + q * NB))
            else:
                sp.dma_start(ring[:, n % 4, :].rearrange("p (k n) -> p k n", k=4),
                             in_q[:, q, :, COL_QA:COL_QA + 2 * NB]).then_inc(loaded[n % 4], 16)

        def in_block(n, col, sa, ada_to, split_to, last_split=True):
            for q in range(2):
                sp.wait_ge(ada_half, ada_to + q)
                load(sa + q, cols(ada_v, q, n * NB))
            for q in range(2):
                if last_split:
                    sp.wait_ge(split_ready, split_to + 8 * q)
                load(2 - sa + q, cols(in_v, q, col))

        for q in range(2):
            sp.wait_ge(ada_half, 14 + q)
            load(q, cols(ada_v, q, ADA_FIRST * NB))
        sp.wait_ge(ada_half, 16)
        load(2, cols(in_v, 0, COL_KA))
        sp.wait_ge(split_ready, U_BLOCKS)
        load(3, cols(in_v, 1, COL_KA))
        for b0, n, col in ((1, 1, COL_KA + NB), (2, 2, COL_QB), (4, 2, COL_VA)):
            with sp.Fori(b0, b0 + n) as b:
                in_block(b + ADA_FIRST, b * NB + (col - b0 * NB), 0, b * 2 + (2 * ADA_FIRST - 1),
                         b * 16 + (U_BLOCKS - 8))
        for n in range(6):
            b = 6
            if n < 2:
                sp.wait_ge(ada_half, 2 * (ADA_FIRST + b) - 1 + n)
                load(n, cols(ada_v, n, (ADA_FIRST + b) * NB))
            elif n < 4:
                sp.wait_ge(split_ready, U_BLOCKS + 16 * (b - 1) + 8 * (n - 1))
                load(n, cols(in_v, n - 2, COL_KVB))
            else:
                sp.wait_ge(ada_half, 2 * (ADA_FIRST + b) + n - 3)
                load(n - 4, cols(ada_v, n - 4, (ADA_FIRST + b + 1) * NB))
        for q in range(2):
            sp.wait_ge(split_ready, U_GATES - 8 + 8 * q)
            load(2 + q, cols(ada_v, q, 16 * NB))
        for q in range(2):
            sp.wait_ge(ada_half, 31 + q)
            load(q, cols(in_v, q, COL_G))
        with sp.Fori(1, 8) as g:
            in_block(g + 16, g * NB + COL_G, 2, g * 2 + 31, g * 16 + (U_GATES - 8))
        def expert_chunk(e, q):
            if q < 4:
                return (gate_v if q % 2 == 0 else up_v)[e, :, q // 2, :]
            return down_v[e, q - 4, :, :, :]

        for n in range(16):
            slot_n = (2 + n) % 4
            if n == 12:
                sp.wait_ge(split_used, U_O_END + CREDIT)
                sp.wait_ge(yT_ready, DB * TT)
                for m in range(2):
                    load(ORDER[m], expert_chunk(0, m))
            if n < 2:
                sp.wait_ge(ada_half, 2 * ADA_BLOCKS - 1 + n)
            else:
                sp.wait_ge(split_ready, U_IN_END + 8 * (n - 3))
            if n < 8:
                v = oA_v if n % 2 == 0 else oB_v
                load(slot_n, v[:, :, (n // 2) * NB:(n // 2 + 1) * NB])
            else:
                load(slot_n, cols(out_v, n % 2, ((n - 8) // 2) * NB))

        def used(pair2, m):
            r, q = m // 12, m % 12
            if q < 8:
                sp.wait_ge(gu_half, pair2 * 4 + (4 * r + q // 2 + 1))
            elif q < 10:
                sp.wait_ge(down_half, pair2 + (r + 1))
            else:
                sp.wait_ge(y_done, pair2 * 4 + (4 * r + 4))

        def expert_step(i, first=False, last=False):
            for m in range(24):
                s, _ = e_chunk(m)
                if m == 8 and first:
                    sp.wait_ge(first_gate, 1)
                elif m >= 8:
                    used(i * 2, m - 8)
                elif not first:
                    used(i * 2 - 2, m + 16)
                elif m < 2:
                    continue
                elif m < 6:
                    sp.wait_ge(split_ready, U_IN_END + 8 * (11 + m))
                else:
                    sp.wait_ge(split_used, U_END + CREDIT)
                r, q = m // 12, m % 12
                e, part = (q // 4, q % 4) if q < 8 else (q % 2, 4 + (q - 8) // 2)
                if last and m >= 22:
                    continue
                load(s, expert_chunk(i * 4 + (2 * r + e), part))

        expert_step(0, True)
        with sp.Fori(1, E // 4 - 1) as i:
            expert_step(i)
        expert_step(E // 4 - 1, last=True)
        for n, (nb0, nb1) in enumerate(PIECES):
            for m in (22, 23):
                s, cut = e_chunk(m)[0], slice(nb0 * NB, nb1 * NB)
                sp.dma_start(ring[:, s, :].rearrange("p (c d) -> p c d", c=2)[:, :, cut],
                             expert_chunk(E - 2 + m % 2, 5)[:, :, cut])\
                    .then_inc(piece_loaded[n] if n < 2 else loaded[s], 16)
        sp.wait_ge(gu_half, 4 * LAST + 3)
        sp.dma_start(rowGf[:, :], mod_rows[3:4, :].broadcast_to([P, D])).then_inc(rowf_loaded, 16)

        sp.wait_ge(tables_ready, 2)
        n_over = sp.value_load(whole[0:1, 8:9], min_val=0, max_val=MAX_OVER)
        with sp.If(n_over > 0):
            sp.wait_ge(y_done, 4 * E // 2)
            with sp.Fori(0, n_over) as j:
                sp.wait_ge(ov_go, j + 1)
                e = sp.value_load(whole[0:1, bass.ds(j, 1)], min_val=0, max_val=E - 1)
                for q in range(6):
                    load(OVER_SLOTS[q], expert_chunk(e, q))

        for n in range(DB * TT):
            t, cut = n // DB, slice((n % DB) * NB, (n % DB + 1) * NB)
            sp.wait_ge(fin_ready, n + 1)
            sp.dma_start(out_t[t][:, cut], xres[:, t, cut]).then_inc(stored, 16)
        sp.wait_ge(stored, 16 * DB * TT)

    @block.gpsimd
    def _(pool):
        nc.gpsimd.memset(ident[:, :], 0.0)
        nc.gpsimd.memset(nslope[:, HEADS:HEADS + 2], 0.0)
        for n in range(HEADS):
            nc.gpsimd.memset(nslope[:, n:n + 1], -8.0 * 2.0 ** (-8.0 * (n + 1) / HEADS))
        nc.gpsimd.iota(dist[:, 0, :], pattern=[[-1, P]], base=P, channel_multiplier=1,
                       allow_small_or_imprecise_dtypes=True)
        nc.gpsimd.iota(dist[:, 1, :], pattern=[[-1, P]], base=0, channel_multiplier=1,
                       allow_small_or_imprecise_dtypes=True)
        nc.gpsimd.iota(dist[:, 2, :], pattern=[[-1, P]], base=0, channel_multiplier=1,
                       allow_small_or_imprecise_dtypes=True)
        nc.gpsimd.iota(dist[:, 3, :], pattern=[[-1, P]], base=P, channel_multiplier=1,
                       allow_small_or_imprecise_dtypes=True)
        pool.drain()
        nc.gpsimd.affine_select(out=ident[:, :], in_=ident[:, :], compare_op=ALU.not_equal, fill=1.0, base=0,
                                pattern=[[-1, P]], channel_multiplier=1)
        for n in (1, 2):
            nc.gpsimd.affine_select(out=dist[:, n, :], in_=dist[:, n, :], compare_op=ALU.is_ge, fill=MASKED,
                                    base=0, pattern=[[-1, P]], channel_multiplier=1)
        nc.gpsimd.affine_select(out=dist[:, 3, :], in_=dist[:, 3, :], compare_op=ALU.is_gt, fill=MASKED,
                                base=0, pattern=[[1, P]], channel_multiplier=-1)
        pool.drain().then_inc(const_ready, 1)
        pool.dma_start(sink[:, :], swa_sinks[0:1, :].broadcast_to([P, HEADS])).then_inc(sink_loaded, 16)

        pool.wait_ge(xn_ready, TT)
        nc.gpsimd.memset(qz[:, :, :, :], 0.0)
        pool.drain()
        pool.wait_ge(block_evac, 8)

        def queries(R, r, blk):
            pool.wait_ge(scored, R + 1)
            for hh in range(2):
                nc.gpsimd.tensor_copy(qz[HD * hh:HD * hh + HD, r % 2, hh, :],
                                      qk[HD * hh:HD * hh + HD, bass.ds(blk, 1), :].rearrange("p a t -> p (a t)"))\
                    .then_inc(qz_ready, 1)

        with pool.Fori(0, 4) as i:
            for r in range(4):
                queries(i * 4 + r, r, i * 2 + (r // 2 + (0 if r % 2 == 0 else 16)))

        pool.wait_ge(vecs_rowed, 1)
        pool.dma_start(mod_rows.rearrange("v (k p) -> (v k) p", p=P), vrow[:, :]).then_inc(rows_stored, 16)
        pool.wait_ge(o_scaled, 17)
        pool.wait_ge(ot_evac, 17)
        pool.dma_start(xres[:, :, :], x_v).then_inc(x_again, 16)
        for nb in range(DB - 1):
            pool.wait_ge(gated, 2 * nb + 2)
            for t in range(TT):
                cut = slice(nb * NB, (nb + 1) * NB)
                nc.gpsimd.tensor_tensor(gateA[:, t, cut], gateA[:, t, cut], gateB[:, t, cut], ALU.add)\
                    .then_inc(y_added, 1)
        nc.gpsimd.iota(iota[:, :], pattern=[[1, T]], base=0, channel_multiplier=0,
                       allow_small_or_imprecise_dtypes=True)
        nc.gpsimd.iota(desc[:, :], pattern=[[-1, E]], base=E, channel_multiplier=0,
                       allow_small_or_imprecise_dtypes=True)
        nc.gpsimd.memset(wtok[:, :, :], 0.0)
        nc.gpsimd.memset(rank[:, :, :], 0.0)
        nc.gpsimd.memset(ones[:, :], 1.0)
        nc.gpsimd.memset(logT[:, :], 0.0)
        nc.gpsimd.memset(upper[:, :], 1.0)
        pool.drain()
        for t in range(TT):
            nc.gpsimd.iota(wtok[:, t, 34:35], pattern=[[0, 1]], base=t * P, channel_multiplier=1,
                           allow_small_or_imprecise_dtypes=True)
        nc.gpsimd.affine_select(out=upper[:, :], in_=upper[:, :], compare_op=ALU.is_ge, fill=0.0, base=0,
                                pattern=[[1, P]], channel_multiplier=-1)
        pool.drain().then_inc(rconst_ready, 1)
        pool.dma_start(wr[:, :, 0:GROUPS], w_router_group[0].rearrange("(k p) n -> p k n", p=P))\
            .then_inc(router_loaded, 16)
        pool.dma_start(wr[:, :, GROUPS:36], w_router_expert[0].rearrange("(k p) n -> p k n", p=P))\
            .then_inc(router_loaded, 16)
        pool.dma_start(rbias[:, 0:GROUPS], b_router_group[0:1, :].broadcast_to([P, GROUPS])).then_inc(router_loaded, 16)
        pool.dma_start(rbias[:, GROUPS:36], b_router_expert[0:1, :].broadcast_to([P, E])).then_inc(router_loaded, 16)

        pool.wait_ge(yT_ready, DB * TT)
        pool.wait_ge(rows_stored, 16)
        pool.dma_start(rowGm[:, :], mod_rows[0:1, :].broadcast_to([P, D])).then_inc(rowm_loaded, 16)
        for n, col in ((2, gainF), (1, shiftF)):
            pool.dma_start(col[:, :], mod_rows[n].rearrange("(p k) -> p k", k=KB)).then_inc(colf_loaded, 16)
        pool.wait_ge(y2_evac, DB)
        pool.wait_ge(ssq_done, 2)
        nc.gpsimd.memset(acc[:, :, :], 0.0).then_inc(acc_zero, 1)

    @block.scalar
    def _(sc_e):
        a = nc.scalar
        a_copy = lambda o, i_: a.activation(o, i_, ACT.Copy)

        def squares(n, src, buf):
            for t in range(TT):
                last = a.activation(buf, src[:, t, :], ACT.Square, accum_out=ssq[:, n, t:t + 1])
                sc_e.drain()
            last = sc_e.drain().then_inc(ssq_done, 1)
            sc_e.wait_ge(inv_ready, n + 1)
            a.activation(rstd[:, n, :], inv[:, n, :], ACT.Sqrt).then_inc(rstd_ready, 1)

        sc_e.dma_start(cc[:, 0, :], c[0].rearrange("(p k) -> p k", k=KB)).then_inc(c_loaded, 16)
        sc_e.dma_start(brow[:, :], b_ada[0].rearrange("(k p) -> k p", p=P)).then_inc(rows_loaded, 16)
        for n, g in enumerate((g_pre_mix, g_post_mix, g_pre_ffn, g_post_ffn)):
            sc_e.dma_start(grow[KB * n:KB * (n + 1), :], g[0].rearrange("(k p) -> k p", p=P))\
                .then_inc(rows_loaded, 16)
        sc_e.wait_ge(c_loaded, 16)
        a.activation(cc[:, 1, :], cc[:, 0, :], ACT.Sigmoid).then_inc(c_sig, 1)
        sc_e.wait_ge(x_loaded, 16)
        squares(0, xres, gateA[:, 0, :])

        def ada_out(m):
            sc_e.wait_ge(ada_half, m * 2 + 2)
            sc_e.wait_ge(col_done, m + 1)
            a_copy(mb[:, :], bank[2][:, :]).then_inc(ada_evac, 1)

        def col_out(m, n):
            sc_e.wait_ge(col_done, m + 2)
            a_copy(msum_flat[:, bass.ds(n * 4, 4)], bank[2][:, 0:4]).then_inc(col_evac, 1)

        sc_e.sem_inc(col_evac, 1)
        for q in range(QUARTERS):
            for part in range(2):
                ada_out(2 * q + part)
                col_out(2 * q + part, QUARTERS * part + q)
            sc_e.wait_ge(colA_ready, q + 1)
            for k in range(4 * q, 4 * q + 4):
                if k % 4 == 0:
                    sc_e.wait_ge(xT_evac, 8)
                a.activation(xnT[:, k, :], xnT[:, k, :], ACT.Identity, bias=msum[:, 0, k:k + 1],
                             scale=colA[:, k:k + 1]).then_inc(xnT_mod, 1)

        def block_out(u_end, dst, banks=(0, 1), func=ACT.Copy):
            sc_e.wait_ge(split_used, u_end + CREDIT)
            for t in range(2):
                last = a.activation(dst(t), bank[banks[t]][:, :], func)
            last.then_inc(block_evac, 1)

        for n in range(2):
            block_out(U_BLOCKS, lambda t: qk[:, 4 * n + 2 * t:4 * n + 2 * t + 2, :].rearrange("p a t -> p (a t)"),
                      banks=((0, 1), (3, 4))[n])
        with sc_e.Fori(0, 4) as b:
            ada_out(b + ADA_FIRST)
            col_out(b + ADA_FIRST, b + ADA_FIRST)
            block_out(b * KB + (U_BLOCKS + KB), lambda t: qk[:, bass.ds(b * 4 + (8 + 2 * t), 2), :]
                      .rearrange("p a t -> p (a t)"))
        for n in range(2):
            ada_out(n + 4 + ADA_FIRST)
            col_out(n + 4 + ADA_FIRST, n + 4 + ADA_FIRST)
            block_out(U_BLOCKS + (5 + n) * KB, lambda t: vA[:, t, n * NB:(n + 1) * NB])
        for m in (14, 15):
            ada_out(m)
            col_out(m, m)
        sc_e.wait_ge(split_used, U_GATES + CREDIT)
        for hf in range(2):
            for par in range(2):
                a_copy(kB[HD * hf:HD * hf + HD, par:KV:2, :],
                       bank[0][HD * par:HD * par + HD, :].rearrange("p (b t) -> p b t", b=2))
        a_copy(vB[:, :, :], bank[1][:, :].rearrange("p (t n) -> p t n", t=TT)).then_inc(block_evac, 1)

        sc_e.sem_inc(pt_evac, 1)
        sc_e.wait_ge(sink_loaded, 16)
        sc_e.sem_inc(ot_evac, 1)
        sc_e.sem_inc(aT_evac, 1)
        sc_e.sem_inc(y_evac, 2)

        def exps(R, r, i):
            b = r % 2
            sc_e.wait_ge(nm_ready, R + 1)
            t1, t0 = (slice(0, 256), slice(256, 384)) if b == 0 else (slice(128, 384), slice(0, 128))
            for hh in range(2):
                for t, cut in ((0, t0), (1, t1)):
                    last = a.activation(sc[:, b, hh, cut], sc[:, b, hh, cut], ACT.Exp, scale=0.125,
                                        bias=nm[:, b, hh, t:t + 1], accum_out=den[:, b, hh, t:t + 1])
                if b == 1:
                    head = i * 4 + ((r // 2) * 2 + hh)
                    a.activation(esink[:, b, hh, :], nm[:, b, hh, :], ACT.Exp,
                                        bias=sink[:, bass.ds(head, 1)])
            sc_e.drain().then_inc(exped, 1)

        def pt_out(R, hh):
            sc_e.wait_ge(pt_done, R * 2 + (hh + 3))
            sc_e.wait_ge(pv_done, R * 2 + hh)
            a_copy(pT[:, hh, :], bank[5][:, 0:3 * P]).then_inc(pt_evac, 1)

        def ot_out(R, r, i):
            blk = i * 2 + (r // 2 + (0 if r % 2 == 0 else 16))
            sc_e.wait_ge(ot_done, R + 2)
            a_copy(qk[:, bass.ds(blk, 1), :].rearrange("p a t -> p (a t)"), bank[7][:, 0:T]).then_inc(ot_evac, 1)

        exps(0, 0, 0)
        def gates_step(i, last=False):
            for r in range(4):
                R = i * 4 + r
                for hh in range(2):
                    pt_out(R, hh)
                    if hh == 0 and r % 2 == 0:
                        ada_out(i * 2 + (16 + r // 2))
                if not (last and r == 3):
                    exps(i * 4 + (r + 1), r + 1, i)
                if r % 2 == 0:
                    col_out(i * 2 + (16 + r // 2), i * 2 + (16 + r // 2))
                ot_out(R, r, i)
                if r % 2 == 1:
                    sc_e.wait_ge(split_used, i * 32 + (U_GATES + 16 * (r // 2 + 1) + CREDIT))
                    for t in range(TT):
                        done = a.activation(gates[:, t, bass.ds(i * 2 * NB + (r // 2) * NB, NB)], bank[t][:, :],
                                            ACT.Copy)
                    done.then_inc(block_evac, 1)

        with sc_e.Fori(0, 3) as i:
            gates_step(i)
        gates_step(3, last=True)
        sc_e.wait_ge(block_evac, 17)
        for nb in range(DB):
            for t in range(TT):
                cut = gates[:, t, :].rearrange("p (m n) -> p m n", m=2)[:, :, nb * NB:(nb + 1) * NB]
                last = a.activation(cut, cut, ACT.Sigmoid)
            last.then_inc(gate_ready, 1)
            if nb == 1:
                sc_e.wait_ge(vecs_T, 1)
                a_copy(vrow[:, :], bank[6][0:4 * KB, 0:P]).then_inc(vecs_rowed, 1)

        for nb in range(DB):
            if nb == 2:
                sc_e.wait_ge(split_used, U_O_END + CREDIT)
            for t in range(TT):
                sc_e.wait_ge(yT_done, 2 * nb + t + 1)
                a_copy(hT_hi[:, 4 * nb:4 * nb + 4, t * P:(t + 1) * P],
                       bank[6 + t][:, :].rearrange("p (k q) -> p k q", k=4)).then_inc(yT_hi, 1)
        a.activation(rstd[:, 0, :], inv[:, 0, :], ACT.Sqrt)
        for nb in range(DB):
            sc_e.wait_ge(split_used, U_O_END + 16 * (nb + 1) + CREDIT)
            for t in range(TT):
                a.activation(dump_y[:, 0:NB], bank[Y_BANKS[nb % 2][t]][:, :], ACT.Square,
                             accum_out=ssq_part[:, t, nb:nb + 1])
                sc_e.drain().then_inc(y2_squared, 1)
        sc_e.wait_ge(inv_ready, 2)
        a.activation(rstd[:, 1, :], inv[:, 1, :], ACT.Sqrt).then_inc(rstd_ready, 1)
        for g in range(DB):
            sc_e.wait_ge(x2T_done, g + 1)
            a_copy(x2T[:, 4 * g:4 * g + 4, 0:P], bank[g][:, :].rearrange("p (k q) -> p k q", k=4))\
                .then_inc(x2T_evac, 1)
        for t in range(TT):
            sc_e.wait_ge(x2_ready, DB * (t + 1))
            a.activation(dump_y[:, :], xres[:, t, :], ACT.Square, accum_out=ssq[:, 2, t:t + 1])
            sc_e.drain()
        sc_e.drain().then_inc(ssq_done, 1)
        sc_e.wait_ge(inv_ready, 3)
        a.activation(rstd[:, 2, :], inv[:, 2, :], ACT.Sqrt).then_inc(rstd_ready, 1)
        sc_e.drain()
        for t in range(TT):
            a.activation(h[:, t, :, :], xres[:, t, :].rearrange("p (q k) -> p k q", k=KB), ACT.Copy,
                         scale=rstd[:, 2, t:t + 1]).then_inc(h_ready, 1)
        def gather_out(r1):
            slots_out(r1)
            rows_out(r1, GATHER)

        def slots_out(r1):
            sc_e.wait_ge(slots_done, r1 + 1)
            a_copy(slot[:, :], bank[7][:, 0:36]).then_inc(slots_evac, 1)

        def rows_out(r1, banks):
            for g in range(4):
                sc_e.wait_ge(got_done, r1 * 4 + (g + 1))
                for kk in range(4):
                    k = 4 * g + kk
                    last = a.activation(xeT[:, k, :], bank[banks[g]][:, kk * P:(kk + 1) * P], ACT.Identity,
                                        bias=shiftF[:, k:k + 1], scale=gainF[:, k:k + 1])
                last.then_inc(got_evac, 1)

        sc_e.wait_ge(colf_loaded, 32)
        rows_out(0, FIRST_GATHER)
        sc_e.wait_ge(ex_in, 1)
        a.activation(ex[:, :, :], ex[:, :, :], ACT.Exp).then_inc(ex_done, 1)
        slots_out(0)

        def acc_squares(nb):
            for t in range(TT):
                a.activation(dump_a[:, :], acc[:, t, nb * NB:(nb + 1) * NB], ACT.Square,
                             accum_out=ssq_part[:, t, nb:nb + 1])
                sc_e.drain()

        def pair(r, last=False):
            for e in range(2):
                sc_e.wait_ge(gu_half, r * 4 + 2 * (e + 1))
                sc_e.wait_ge(aT_done, r + 1)
                a.activation(act[:, e, :], bank[e][:, 0:T], ACT.Sigmoid).then_inc(sig_done, 1)
            if not last:
                gather_out(r + 1)
            sc_e.wait_ge(aT_done, r + 2)
            a_copy(actT[:, :, :, :].rearrange("p e c s -> p (e c s)"), bank[2][:, :]).then_inc(aT_evac, 1)
            for nb in range(DB):
                sc_e.wait_ge(y_done, r * 4 + (nb + 1))
                sc_e.wait_ge(comb_done, r * 8 + (2 * nb + 2))
                a_copy(ye[:, nb * NB:(nb + 1) * NB], bank[DOWN[nb]][:, :])\
                    .then_inc(y_evac, 1)
                if last and nb >= 2:
                    sc_e.wait_ge(comb_added, r * 8 + (2 * nb))
                    acc_squares(nb - 2)

        with sc_e.Fori(0, E // 4 - 1) as i:
            for x2 in range(2):
                pair(i * 2 + x2)
        pair(LAST - 1)
        pair(LAST, last=True)
        for nb in (2, 3):
            sc_e.wait_ge(comb_added, LAST * 8 + (2 * nb + 4))
            acc_squares(nb)

        sc_e.wait_ge(tables_ready, 2)
        n_over = sc_e.value_load(whole[0:1, 8:9], min_val=0, max_val=MAX_OVER)
        with sc_e.If(n_over > 0):
            with sc_e.Fori(0, n_over) as j:
                sc_e.wait_ge(ov_got, j + 1)
                a_copy(slot[0:CAP, 0:2], bank[7][0:CAP, 0:2])
                for k in range(KB):
                    last = a.activation(xeT[:, k, 0:CAP], bank[5 + k // 8][:, (k % 8) * CAP:(k % 8 + 1) * CAP],
                                        ACT.Identity, bias=shiftF[:, k:k + 1], scale=gainF[:, k:k + 1])
                last.then_inc(ov_in, 1)
                sc_e.wait_ge(ov_gu, j + 1)
                a.activation(act[:, 0, :], bank[0][:, 0:T], ACT.Sigmoid).then_inc(ov_sig, 1)
                sc_e.wait_ge(ov_aT, j + 1)
                a_copy(actT[:, 0, :, :].rearrange("p c s -> p (c s)"), bank[2][:, 0:T]).then_inc(ov_aTe, 1)
                sc_e.wait_ge(ov_y, j + 1)
                for nb in range(DB):
                    last = a_copy(ye[0:CAP, nb * NB:(nb + 1) * NB], bank[3 + nb][0:CAP, :])
                last.then_inc(ov_ye, 1)
            sc_e.wait_ge(ov_done, 1)
            for nb in range(DB):
                acc_squares(nb)
        sc_e.drain().then_inc(ssq_done, 1)
        sc_e.wait_ge(inv_ready, 4)
        a.activation(rstd[:, 3, :], inv[:, 3, :], ACT.Sqrt).then_inc(rstd_ready, 1)

    @block.tensor
    def _(pe):
        mm, tr = nc.tensor.matmul, nc.tensor.transpose
        pe.sem_inc(split_used, CREDIT)
        pe.sem_inc(scored, 2)
        pe.sem_inc(pt_done, 2)
        pe.sem_inc(pv_done, 1)
        pe.sem_inc(ot_done, 1)
        pe.sem_inc(aT_done, 1)
        pe.sem_inc(col_done, 1)
        pe.sem_inc(comb_done, 8)

        def ada(m, at):
            pe.wait_ge(col_evac, m + 1)
            for hf, (s, count) in enumerate(at):
                pe.wait_ge(loaded[s], count)
                for kk in range(8):
                    k = hf * 8 + kk
                    g = kk % 4
                    last = mm(bank[2][32 * g:32 * g + 32, :], condb[:, k, :], ring[:, s, kk * NB:(kk + 1) * NB],
                              start=(k < 4), stop=(k >= 12))
                last.then_inc(ada_half, 1)

        def col(m):
            pe.wait_ge(ada_evac, m + 1)
            for q in range(4):
                last = mm(bank[2][:, q:q + 1], mb[:, q * P:(q + 1) * P], sel[:, :], start=True, stop=True)
            last.then_inc(col_done, 1)

        def split_mm(o_of, hi, lo, k, b, start, stop, w_hi=w_hi, w_lo=w_lo):
            for t in range(TT):
                cut = slice(t * P, (t + 1) * P)
                mm(o_of(t), hi[:, k, cut], w_hi[:, b, :], start=start, stop=False)
                mm(o_of(t), hi[:, k, cut], w_lo[:, b, :], start=False, stop=False)
                last = mm(o_of(t), lo[:, k, cut], w_hi[:, b, :], start=False, stop=stop)
            last.then_inc(split_used, 1)

        def split_mm_T(outs, k, b, start, stop):
            for blk in range(4):
                o = outs[blk // 2][:, (blk % 2) * T:(blk % 2 + 1) * T]
                cut = slice(blk * P, (blk + 1) * P)
                mm(o, w_hi[:, b, cut], hT_hi[:, k, :], start=start and blk % 2 == 0, stop=False,
                   skip_group_check=True)
                mm(o, w_hi[:, b, cut], hT_lo[:, k, :], start=False, stop=False, skip_group_check=True)
                last = mm(o, w_lo[:, b, cut], hT_hi[:, k, :], start=False, stop=stop, skip_group_check=True)
            last.then_inc(split_used, 1)

        def keep_busy(n):
            for _ in range(n):
                mm(bank[7][:, 0:P], ident[:, :], ident[:, :], start=True, stop=True)

        pe.wait_ge(cond_ready, 1)
        for q in range(QUARTERS):
            for part in range(2):
                ada(2 * q + part, [front(5 * q + 2 * part), front(5 * q + 2 * part + 1)])
                if q == 0 and part == 0:
                    pe.wait_ge(rows_loaded, 80)
                    tr(bank[7][:, 0:6 * KB], brow[:, :], ident[0:6 * KB, 0:6 * KB])
                    tr(bank[7][:, P:P + 4 * KB], grow[:, :], ident[0:4 * KB, 0:4 * KB]).then_inc(rows_T, 1)
                    for g in range(8):
                        t, kq = g // 4, g % 4
                        if g % 4 == 0:
                            pe.wait_ge(xn_ready, t + 1)
                        if g >= 2:
                            pe.wait_ge(xT_evac, g - 1)
                        for n in range(4):
                            last = tr(bank[5 + g % 2][:, n * P:(n + 1) * P], xn[:, t, 4 * kq + n, :], ident[:, :])
                        last.then_inc(xT_done, 1)
                col(2 * q + part)
            pe.wait_ge(xT_evac, 8)
            keep_busy(24)
            pe.wait_ge(hT_ready, q + 1)
            for n in range(8):
                pe.wait_ge(split_ready, 8 * q + n + 1)
                k = 4 * q + n // 2
                split_mm_T((bank[0:2], bank[3:5])[n % 2], k, n % SPLITS, k == 0, k == KB - 1)

        def in_steps(u, k0, k1, transposed):
            for k in range(k0, k1):
                pe.wait_ge(split_ready, u + (k + 1))
                if transposed:
                    split_mm_T(bank[0:2], k, k % SPLITS, k == 0, k == KB - 1)
                else:
                    split_mm(lambda t: bank[t][:, :], hT_hi, hT_lo, k, k % SPLITS, k == 0, k == KB - 1)

        def in_block(b, transposed):
            ada(b + ADA_FIRST, [(0, b * 16 + 16 * (C_BLOCKS // 4 + 1)), (1, b * 16 + 16 * (C_BLOCKS // 4 + 1))])
            pe.wait_ge(block_evac, b + 2)
            in_steps(b * KB + U_BLOCKS, 0, 8, transposed)
            col(b + ADA_FIRST)
            in_steps(b * KB + U_BLOCKS, 8, KB, transposed)

        with pe.Fori(0, 4) as b:
            in_block(b, True)
        with pe.Fori(4, 6) as b:
            in_block(b, False)
        ada(14, [front(C_KV), front(C_KV + 1)])
        pe.wait_ge(block_evac, 8)
        for k in range(KB):
            if k == 8:
                col(14)
            pe.wait_ge(split_ready, U_BLOCKS + 6 * KB + k + 1)
            b = k % SPLITS
            for blk in range(2):
                o = bank[0][:, blk * T:(blk + 1) * T]
                cut = slice(blk * P, (blk + 1) * P)
                for n, (w, hh) in enumerate(((w_hi, hT_hi), (w_hi, hT_lo), (w_lo, hT_hi))):
                    mm(o, w[:, b, cut], hh[:, k, :], start=(k == 0 and blk == 0 and n == 0), stop=(k == KB - 1),
                       skip_group_check=True)
            for t in range(TT):
                o = bank[1][:, t * T:(t + 1) * T]
                cut = slice(t * P, (t + 1) * P)
                for n, (w, hh) in enumerate(((w_hi, hT_hi), (w_hi, hT_lo), (w_lo, hT_hi))):
                    last = mm(o, hh[:, k, cut], w[:, b, 2 * P:4 * P], start=(k == 0 and t == 0 and n == 0),
                              stop=(k == KB - 1), skip_group_check=True)
            last.then_inc(split_used, 1)
        ada(15, [front(C_KV + 4), front(C_KV + 5)])
        col(15)

        SB = (3, 4)

        def scores(R, r, i):
            b = r % 2
            pe.wait_ge(qz_ready, R * 2 + 2)
            pe.wait_ge(biased, R + 1)
            for hh in range(2):
                o = bank[SB[hh]]
                q0, q1 = qz[:, b, hh, 0:P], qz[:, b, hh, P:T]
                if b == 0:
                    kk = i * 2 + (8 + r // 2)
                    key = lambda lo_, hi_: qk[:, bass.ds(kk, 1), lo_:hi_].rearrange("p a t -> p (a t)")
                    mm(o[:, 0:T], q1, key(0, T), start=True, stop=True)
                    last = mm(o[:, T:3 * P], q0, key(0, P), start=True, stop=True)
                else:
                    key = lambda lo_, hi_: kB[:, bass.ds(i, 1), lo_:hi_].rearrange("p a t -> p (a t)")
                    mm(o[:, 0:P], q0, key(0, P), start=True, stop=True)
                    mm(o[:, P:T], q1, key(P, T), start=True, stop=True)
                    last = mm(o[:, T:3 * P], q1, key(0, P), start=True, stop=True)
            last.then_inc(scored, 1)

        def transposed_p(R, r, hh):
            if hh == 0:
                pe.wait_ge(exped, R + 1)
            pe.wait_ge(pt_evac, R * 2 + (hh + 1))
            for n in range(3):
                last = tr(bank[5][:, n * P:(n + 1) * P], sc[:, r % 2, hh, n * P:(n + 1) * P], ident[:, :])
            last.then_inc(pt_done, 1)

        def pv(R, r, i, hh):
            b = r % 2
            pe.wait_ge(pt_evac, R * 2 + (hh + 2))
            pe.wait_ge(o_scaled, R + 1)
            if b == 0:
                at = i * (4 * HD) + ((r // 2) * 2 * HD + hh * HD)
                val = lambda t: vA[:, t, bass.ds(at, HD)]
                cuts = ((0, ((2, 0),)), (1, ((0, 0), (1, 1))))
            else:
                val = lambda t: vB[:, t, bass.ds(i * HD, HD)]
                cuts = ((0, ((0, 0),)), (1, ((1, 1), (2, 0))))
            for t, parts in cuts:
                o = bank[6][:, (hh * 2 + t) * HD:(hh * 2 + t + 1) * HD]
                for n, (pb, kt) in enumerate(parts):
                    last = mm(o, pT[:, hh, pb * P:(pb + 1) * P], val(kt), start=(n == 0),
                              stop=(n == len(parts) - 1))
            last.then_inc(pv_done, 1)

        def transposed_o(R):
            pe.wait_ge(o_scaled, R + 2)
            pe.wait_ge(ot_evac, R + 1)
            for t in range(TT):
                last = tr(bank[7][:, t * P:(t + 1) * P], osb[:, t, :, :].rearrange("p h d -> p (h d)"), ident[:, :])
            last.then_inc(ot_done, 1)

        scores(0, 0, 0)
        def gates_step(i, last=False):
            for half in range(2):
                m = i * 2 + (16 + half)
                uses_g = i * 32 + 16 * (half + 1 + C_GATES // 4)
                u = i * 32 + (U_GATES + 16 * half)
                ada(m, [(2, uses_g), (3, uses_g)])
                pe.wait_ge(block_evac, i * 2 + (9 + half))
                for w in range(2):
                    r = 2 * half + w
                    R = i * 4 + r
                    transposed_p(R, r, 0)
                    in_steps(u, 8 * w, 8 * w + 2, False)
                    transposed_p(R, r, 1)
                    pv(R, r, i, 0)
                    in_steps(u, 8 * w + 2, 8 * w + 3, False)
                    if not (last and r == 3):
                        scores(R + 1, r + 1, i)
                    in_steps(u, 8 * w + 3, 8 * w + 4, False)
                    pv(R, r, i, 1)
                    if w == 0:
                        col(m)
                    in_steps(u, 8 * w + 4, 8 * w + 7, False)
                    transposed_o(R)
                    in_steps(u, 8 * w + 7, 8 * w + 8, False)

        with pe.Fori(0, 3) as i:
            gates_step(i)
        gates_step(3, last=True)

        def y_transposed(nb):
            for t in range(TT):
                pe.wait_ge(y_added, 2 * nb + t + 1)
                if nb > 0:
                    pe.wait_ge(yT_ready, 2 * nb + t - 1)
                for q in range(4):
                    last = tr(bank[6 + t][:, q * P:(q + 1) * P], gateA[:, t, (4 * nb + q) * P:(4 * nb + q + 1) * P],
                              ident[:, :])
                last.then_inc(yT_done, 1)

        for n in range(2 * DB):
            m = n % 2
            hi, lo = ((oA_hi, oA_lo), (hT_hi, hT_lo))[m]
            if n < 2:
                pe.wait_ge(oT_split, m + 1)
            if n == 2:
                pe.wait_ge(block_evac, 17)
                pe.wait_ge(vecs_ready, 1)
                tr(bank[6][0:4 * KB, 0:P], vecs[:, :, :].rearrange("p v k -> p (v k)"), ident[:, :])\
                    .then_inc(vecs_T, 1)
            if n >= 3:
                pe.wait_ge(gated, n - 2)
            if n == 3:
                pe.wait_ge(vecs_rowed, 1)
            for kk in range(8):
                if kk == 4 and n % 2 == 1 and n >= 3:
                    y_transposed(n // 2 - 1)
                pe.wait_ge(split_ready, U_IN_END + n * 8 + kk + 1)
                split_mm(lambda t: bank[O_BANKS[n % 3][t]][:, :], hi, lo, m * 8 + kk if m else kk, kk % SPLITS,
                         kk == 0, kk == 7)
        pe.wait_ge(gated, 2 * DB - 2)
        for nb in range(DB):
            if nb == 3:
                pe.wait_ge(shift_in, 1)
                pe.wait_ge(rconst_ready, 1)
                mm(bank[6][:, 0:36], ones[:, :], swp[:, :], start=True, stop=True).then_inc(shift_done, 1)
            if nb >= 2:
                pe.wait_ge(y2_evac, nb - 1)
            for k in range(KB):
                if nb == 0:
                    if k == 8:
                        y_transposed(DB - 1)
                    pe.wait_ge(yT_ready, 2 * (k // 4 + 1))
                pe.wait_ge(split_ready, U_O_END + nb * 16 + k + 1)
                split_mm(lambda t: bank[Y_BANKS[nb % 2][t]][:, :], hT_hi, hT_lo, k, k % SPLITS, k == 0,
                         k == KB - 1, wo_hi, wo_lo)

        keep_busy(12)
        pe.wait_ge(shift_in, 2)
        def logits(t, g):
            pe.wait_ge((x2T_evac, x2T_evac1)[t], g + 1)
            for k in range(4 * g, 4 * g + 4):
                at = 64 * (k % 2)
                last = mm(bank[t][at:at + 36, 0:P], wr[:, k, :], x2T[:, k, t * P:(t + 1) * P],
                          start=(k < 2), stop=(k >= KB - 2))
            if g == 3:
                last.then_inc(logT_done, 1)

        for g in range(8):
            t, kq = g // 4, g % 4
            pe.wait_ge(x2_ready, g + 1)
            for q in range(4):
                k = 4 * kq + q
                last = tr(bank[g][:, q * P:(q + 1) * P], xres[:, t, k * P:(k + 1) * P], ident[:, :])
            last.then_inc(x2T_done, 1)
            if g >= 4:
                logits(0, g - 4)
        for g in range(4):
            logits(1, g)
        for t in range(TT):
            pe.wait_ge(logT_evac, 2 * (t + 1))
            mm(bank[2][:, t * 64:t * 64 + 36], logT[0:100, t * P:(t + 1) * P], fold[0:100, :], start=True, stop=True)\
                .then_inc(logits_done, 1)
        keep_busy(26)
        pe.wait_ge(hot_ready, 1)
        pe.wait_ge(rconst_ready, 1)
        mm(bank[5][:, 0:E], upper[:, :], em[:, 0, :], start=True, stop=True)
        mm(bank[5][:, E:2 * E], ones[:, :], em[:, 0, :], start=True, stop=False)
        mm(bank[5][:, E:2 * E], upper[:, :], em[:, 1, :], start=False, stop=True).then_inc(rank_done, 1)
        mm(bank[2][:, 2 * E:3 * E], ones[:, :], em[:, 0, :], start=True, stop=False)
        mm(bank[2][:, 2 * E:3 * E], ones[:, :], em[:, 1, :], start=False, stop=True).then_inc(count_done, 1)

        pe.wait_ge(picked, 1)

        def gather(r1):
            pe.wait_ge(picked, r1 + 1)
            pe.wait_ge(slots_evac, r1)
            slots(r1)
            for g in range(4):
                if g == 2:
                    pe.wait_ge(slots_evac, r1 + 1)
                if g == 3:
                    pe.wait_ge(got_evac, r1 * 4 + 1)
                rows(bank[GATHER[g]], g)

        def slots(r1):
            for t in range(TT):
                last = mm(bank[7][:, 0:36], pick[:, t, :, :].rearrange("p e s -> p (e s)"), wtok[:, t, :],
                          start=(t == 0), stop=(t == TT - 1))
            last.then_inc(slots_done, 1)

        def rows(o, g):
            for kk in range(4):
                for t in range(TT):
                    last = mm(o[:, kk * P:(kk + 1) * P], h[:, t, 4 * g + kk, :],
                              pick[:, t, :, :].rearrange("p e s -> p (e s)"), start=(t == 0), stop=(t == TT - 1))
            last.then_inc(got_done, 1)

        def uses(s, i3, more):
            return i3 * 48 + 16 * (FRONT_USES[s] + more)

        def gate_up(slots, o, got, before=None):
            for hf in range(2):
                if before is not None and hf == 0:
                    for m, (s, count) in enumerate(slots[0:2]):
                        pe.wait_ge(loaded[s], count)
                        for k in range(8):
                            if m == 0 and k % 4 == 0:
                                before(k // 4)
                            for g in range(2):
                                last = mm(o[CAP * g:CAP * g + CAP, m * T:(m + 1) * T], got(k),
                                          ring[:, s, k * NB + g * T:k * NB + (g + 1) * T],
                                          start=(m == 0 and k == 0), stop=False, skip_group_check=True)
                        if m == 0:
                            last.then_inc(first_gate, 1)
                    yield last
                    continue
                for s in slots[2 * hf:2 * hf + 2]:
                    pe.wait_ge(loaded[s[0]], s[1])
                s = slots[2 * hf][0]
                both = ring[:, s:s + 2, :].rearrange("p m (k n) -> p m k n", k=8)
                for kk in range(8):
                    k = hf * 8 + kk
                    if before is not None and k % 4 == 0:
                        before(k // 4)
                    for g in range(2):
                        last = mm(o[CAP * g:CAP * g + CAP, :].rearrange("p (m n) -> p m n", m=2), got(k),
                                  both[:, :, kk, g * T:(g + 1) * T], start=(k == 0), stop=(k == KB - 1), skip_group_check=before is not None)
                yield last

        def gu_slots(i, x2, e):
            at = [e_chunk(12 * x2 + 4 * e + q) for q in range(4)]
            return [(s, uses(s, i, more)) for s, more in at]

        def got(e):
            return lambda k: xeT[:, k, CAP * e:CAP * e + CAP]

        def first_rows(g):
            if g == 0:
                pe.wait_ge(h_ready, TT)
                rows(bank[FIRST_GATHER[0]], 0)
            if g < 3:
                rows(bank[FIRST_GATHER[g + 1]], g + 1)
            pe.wait_ge(got_evac, g + 1)

        def down_mm(o, nb, g, slots2):
            for cb in range(2):
                for e in range(2):
                    last = mm(o[CAP * e:CAP * e + CAP, :], actT[:, e, cb, CAP * g:CAP * g + CAP],
                              ring[:, slots2[e], cb * D + nb * NB:cb * D + (nb + 1) * NB],
                              start=(g == 0 and cb == 0), stop=(g == 1 and cb == 1))
            return last

        def pair(r, i, x2, first=False, final=False):
            for e in range(2):
                pe.wait_ge(act_ready, r * 2 + (e + 1))
                if first and e == 0:
                    for last in gate_up(gu_slots(i, x2, e), bank[e], got(e), first_rows):
                        last.then_inc(gu_half, 1)
                    pe.wait_ge(tables_ready, 1)
                    slots(0)
                    continue
                if e == 0:
                    pe.wait_ge(got_evac, r * 4 + 4)
                for last in gate_up(gu_slots(i, x2, e), bank[e], got(e)):
                    last.then_inc(gu_half, 1)
            if final:
                keep_busy(8)
            else:
                gather(r + 1)
            for e in range(2):
                pe.wait_ge(act_ready, r * 2 + (e + 3))
                if e == 0:
                    pe.wait_ge(aT_evac, r + 1)
                for cb in range(2):
                    last = tr(bank[2][:, (2 * e + cb) * P:(2 * e + cb + 1) * P], act[:, e, cb * P:(cb + 1) * P],
                              ident[:, :])
            last.then_inc(aT_done, 1)
            pe.wait_ge(aT_evac, r + 2)
            if not final:
                pe.wait_ge(got_evac, r * 4 + 8)
            down = [e_chunk(12 * x2 + 8 + q) for q in range(4)]

            def combine(nb):
                if nb == 0:
                    pe.wait_ge(send_ready, r + 1)
                pe.wait_ge(y_evac, r * 4 + (nb + 3))
                for t in range(TT):
                    pe.wait_ge(comb_added, r * 8 + (nb * 2 + t + 1))
                    mm(bank[5 + t][:, :], send[:, t * P:(t + 1) * P], ye[:, nb * NB:(nb + 1) * NB],
                       start=True, stop=True).then_inc(comb_done, 1)

            def down_loaded(q0):
                for s, m in down[q0:q0 + 2]:
                    pe.wait_ge(loaded[s], uses(s, i, m))

            at = lambda g: [down[2 * g][0], down[2 * g + 1][0]]
            down_loaded(0)
            for nb in range(DB):
                last = down_mm(bank[DOWN[nb]], nb, 0, at(0))
            last.then_inc(down_half, 1)
            if not final:
                down_loaded(2)
            for nb in range(DB):
                if final:
                    if nb in (0, 2):
                        pe.wait_ge(piece_loaded[nb // 2], 32)
                    elif nb == 3:
                        down_loaded(2)
                down_mm(bank[DOWN[nb]], nb, 1, at(1)).then_inc(y_done, 1)
                if nb > 0:
                    combine(nb - 1)
            combine(DB - 1)

        for x2 in range(2):
            pair(x2, 0, x2, first=(x2 == 0))
        with pe.Fori(1, E // 4 - 1) as i:
            for x2 in range(2):
                pair(i * 2 + x2, i, x2)
        for x2 in range(2):
            pair(LAST - 1 + x2, E // 4 - 1, x2, final=(x2 == 1))

        pe.wait_ge(tables_ready, 2)
        n_over = pe.value_load(whole[0:1, 8:9], min_val=0, max_val=MAX_OVER)
        with pe.If(n_over > 0):
            pe.wait_ge(y_evac, 2 * E + 2)
            with pe.Fori(0, n_over) as j:
                pe.wait_ge(ov_pick, j + 1)
                for t in range(TT):
                    mm(bank[7][0:CAP, 0:2], pick[:, t, 0, :], tover[:, t, :], start=(t == 0), stop=(t == TT - 1))
                for k in range(KB):
                    for t in range(TT):
                        last = mm(bank[5 + k // 8][:, (k % 8) * CAP:(k % 8 + 1) * CAP], h[:, t, k, :],
                                  pick[:, t, 0, :], start=(t == 0), stop=(t == TT - 1))
                last.then_inc(ov_got, 1)
                pe.wait_ge(ov_in, j + 1)
                over_uses = lambda q: j * 16 + 16 * (FRONT_USES[OVER_SLOTS[q]] + 25)
                sl = [(OVER_SLOTS[q], over_uses(q)) for q in range(4)]
                for last in gate_up(sl, bank[0], lambda k: xeT[:, k, 0:CAP]):
                    pass
                last.then_inc(ov_gu, 1)
                pe.wait_ge(ov_act, j + 1)
                for cb in range(2):
                    last = tr(bank[2][:, cb * P:(cb + 1) * P], act[:, 0, cb * P:(cb + 1) * P], ident[:, :])
                last.then_inc(ov_aT, 1)
                pe.wait_ge(ov_aTe, j + 1)
                for q in (4, 5):
                    pe.wait_ge(loaded[OVER_SLOTS[q]], over_uses(q))
                for nb in range(DB):
                    for g in range(2):
                        for cb in range(2):
                            last = mm(bank[3 + nb][0:CAP, :], actT[:, 0, cb, CAP * g:CAP * g + CAP],
                                      ring[:, OVER_SLOTS[4 + g], cb * D + nb * NB:cb * D + (nb + 1) * NB],
                                      start=(g == 0 and cb == 0), stop=(g == 1 and cb == 1))
                last.then_inc(ov_y, 1)
                pe.wait_ge(ov_ye, j + 1)
                for nb in range(DB):
                    for t in range(TT):
                        last = mm(bank[2 * nb + t][:, :], send[0:CAP, t * P:(t + 1) * P],
                                  ye[0:CAP, nb * NB:(nb + 1) * NB], start=True, stop=True)
                last.then_inc(ov_comb, 1)

    @block.vector
    def _(dve):
        v = nc.vector

        def inverse(n, squared):
            dve.wait_ge(ssq_done, squared)
            v.tensor_scalar(inv[:, n, :], ssq[:, n, :], 1.0 / D, EPS, ALU.mult, ALU.add)
            dve.drain()
            v.reciprocal(inv[:, n, :], inv[:, n, :]).then_inc(inv_ready, 1)
            dve.wait_ge(rstd_ready, n + 1)

        dve.sem_inc(biased, 1)
        dve.sem_inc(o_scaled, 1)
        dve.sem_inc(act_ready, 2)
        dve.sem_inc(comb_added, 2)
        dve.wait_ge(const_ready, 1)
        v.tensor_reduce(sel[:, :], ident[:, 0:97:32], AX.X, ALU.add)
        dve.wait_ge(c_sig, 1)
        v.tensor_tensor(cc[:, 2, :], cc[:, 0, :], cc[:, 1, :], ALU.mult)
        dve.drain()
        v.tensor_copy(condb[:, :, :], cc[:, 2, :].unsqueeze(2).broadcast_to([P, KB, 32])).then_inc(cond_ready, 1)
        inverse(0, 1)
        for t in range(TT):
            v.tensor_scalar(xn[:, t, :, :], xres[:, t, :].rearrange("p (k q) -> p k q", k=KB),
                            rstd[:, 0, t:t + 1], None, ALU.mult).then_inc(xn_ready, 1)
        dve.wait_ge(rows_T, 1)
        v.tensor_copy(badac_flat[:, :], bank[7][:, 0:6 * KB])
        v.tensor_copy(gains_flat[:, :], bank[7][:, P:P + 4 * KB])
        for g in range(8):
            t, kq = g // 4, g % 4
            dve.wait_ge(xT_done, g + 1)
            v.tensor_copy(xnT[:, 4 * kq:4 * kq + 4, t * P:(t + 1) * P],
                          bank[5 + g % 2][:, :].rearrange("p (k q) -> p k q", k=4)).then_inc(xT_evac, 1)

        def split_steps(s, count, u, k0=0, k1=8, w_hi=w_hi, w_lo=w_lo):
            if k0 == 0:
                dve.wait_ge(loaded[s], count)
            hi_of = lambda k: w_hi[:, k % SPLITS, :]
            for k in range(k0, k1 + 1):
                if k < k1:
                    dve.wait_ge(split_used, u + (k + 1))
                    v.tensor_copy(hi_of(k), ring[:, s, k * NB:(k + 1) * NB]).then_inc(hi_done, 1)
                if k > k0:
                    dve.wait_ge(hi_done, u + k)
                    v.tensor_tensor(w_lo[:, (k - 1) % SPLITS, :], ring[:, s, (k - 1) * NB:k * NB],
                                    hi_of(k - 1).bitcast(F32), ALU.subtract).then_inc(split_ready, 1)

        for q in range(QUARTERS):
            cut = slice(4 * q, 4 * q + 4)
            dve.wait_ge(col_evac, 2 * q + 3)
            v.tensor_tensor(msum[:, 0:2, cut], msum[:, 0:2, cut], badac[:, 0:2, cut], ALU.add)
            dve.drain()
            v.scalar_tensor_tensor(colA[:, cut], msum[:, 1, cut], 1.0, gains[:, 0, cut], ALU.add, ALU.mult)\
                .then_inc(colA_ready, 1)
            dve.wait_ge(xnT_mod, 4 * (q + 1))
            v.tensor_copy(hT_hi[:, cut, :], xnT[:, cut, :])
            dve.drain()
            v.tensor_tensor(hT_lo[:, cut, :], xnT[:, cut, :], hT_hi[:, cut, :].bitcast(F32), ALU.subtract)\
                .then_inc(hT_ready, 1)
            split_steps(*front(5 * q + 4), 8 * q)
        with dve.Fori(0, 6) as b:
            for q in range(2):
                split_steps(2 + q, b * 16 + 16 * (C_BLOCKS // 4 + 1), b * KB + (U_BLOCKS + 8 * q))
        for q in range(2):
            split_steps(*front(C_KV + 2 + q), U_BLOCKS + 6 * KB + 8 * q)
        dve.wait_ge(sink_loaded, 16)
        v.tensor_scalar(nsink[:, :], sink[:, :], -1.0, None, ALU.mult)
        dve.drain()

        SB = (3, 4)
        dve.wait_ge(const_ready, 1)

        def bias_max(R, r, i):
            b = r % 2
            dve.wait_ge(scored, R + 3)
            dve.wait_ge(pt_done, R * 2)
            for hh in range(2):
                head = i * 4 + ((r // 2) * 2 + hh)
                last = v.scalar_tensor_tensor(sc[:, b, hh, :], dist[:, b:b + 3, :].rearrange("p a k -> p (a k)"),
                                              nslope[:, bass.ds(head, 1)], bank[SB[hh]][:, 0:3 * P],
                                              ALU.mult, ALU.add)
            last.then_inc(biased, 1)
            dve.drain()
            t1, t0 = (slice(0, 256), slice(256, 384)) if b == 0 else (slice(128, 384), slice(0, 128))
            for t, cut in ((0, t0), (1, t1)):
                v.tensor_reduce(mx[:, b, :, t], sc[:, b, :, cut], AX.X, ALU.max)
            dve.drain()
            if b == 0:
                v.tensor_scalar(nm[:, b, :, :], mx[:, b, :, :], -0.125, None, ALU.mult).then_inc(nm_ready, 1)
            else:
                v.tensor_scalar(nm[:, b, :, :], mx[:, b, :, :], -0.125, None, ALU.mult)
                dve.drain()
                head = i * 4 + (r // 2) * 2
                v.tensor_tensor(nm[:, b, :, :], nm[:, b, :, :],
                                nsink[:, bass.ds(head, 2)].unsqueeze(2).broadcast_to([P, 2, TT]), ALU.min)\
                    .then_inc(nm_ready, 1)

        def o_scale(R, r):
            b = r % 2
            dve.wait_ge(exped, R + 1)
            if b == 1:
                v.tensor_tensor(den[:, b, :, :], den[:, b, :, :], esink[:, b, :, :], ALU.add)
                dve.drain()
            v.reciprocal(den[:, b, :, :], den[:, b, :, :])
            dve.drain()
            dve.wait_ge(pv_done, R * 2 + 3)
            dve.wait_ge(ot_done, R + 1)
            for hh in range(2):
                last = v.tensor_tensor(osb[:, :, hh, :],
                                       bank[6][:, hh * P:(hh + 1) * P].rearrange("p (t d) -> p t d", t=TT),
                                       den[:, b, hh, :].unsqueeze(2).broadcast_to([P, TT, HD]), ALU.mult)
            last.then_inc(o_scaled, 1)

        bias_max(0, 0, 0)
        def o_split(src, hi, lo):
            v.tensor_copy(hi, src)
            dve.drain()
            return v.tensor_tensor(lo, src, hi.bitcast(F32), ALU.subtract)

        def gates_step(i, last=False):
            for r in range(4):
                at = (r % 2, i * 32 + 16 * (r // 2 + 1 + (C_GATES + 2) // 4), i * 32 + (U_GATES + 8 * r))
                if last and r == 3:
                    split_steps(*at, 0, 4)
                    dve.wait_ge(ot_evac, 16)
                    o_split(qk[:, 0:8, :], oA_hi[:, :, :], oA_lo[:, :, :]).then_inc(oT_split, 1)
                    split_steps(*at, 4, 7)
                else:
                    split_steps(*at, 0, 7)
                    bias_max(i * 4 + (r + 1), r + 1, i)
                o_scale(i * 4 + r, r)
                split_steps(*at, 7, 8)

        with dve.Fori(0, 3) as i:
            gates_step(i)
        gates_step(3, last=True)

        def later_vectors():
            dve.wait_ge(col_evac, ADA_BLOCKS + 1)
            v.tensor_tensor(msum[:, 2:6, :], msum[:, 2:6, :], badac[:, 2:6, :], ALU.add)
            dve.drain()
            for n, m, g in ((0, 2, 1), (3, 5, 3)):
                v.tensor_tensor(vecs[:, n, :], msum[:, m, :], gains[:, g, :], ALU.mult)
            v.tensor_copy(vecs[:, 1, :], msum[:, 3, :])
            v.scalar_tensor_tensor(vecs[:, 2, :], msum[:, 4, :], 1.0, gains[:, 2, :], ALU.add, ALU.mult)
            dve.drain().then_inc(vecs_ready, 1)

        def gate_out(n):
            nb, m = n // 2, n % 2
            dve.wait_ge(gate_ready, nb + 1)
            dve.wait_ge(split_used, U_IN_END + 8 * (n + 1) + CREDIT)
            cut = slice(nb * NB, (nb + 1) * NB)
            for t in range(TT):
                gt = (gateA, gateB)[m][:, t, cut]
                last = v.tensor_tensor(gt, gt, bank[O_BANKS[n % 3][t]][:, :], ALU.mult)
            last.then_inc(gated, 1)
            if n == 2 * DB - 1:
                dve.drain()
                for t in range(TT):
                    v.tensor_tensor(gateA[:, t, cut], gateA[:, t, cut], gateB[:, t, cut], ALU.add)\
                        .then_inc(y_added, 1)

        def y_low(nb):
            for t in range(TT):
                dve.wait_ge(yT_hi, 2 * nb + t + 1)
                cut = (slice(None), slice(4 * nb, 4 * nb + 4), slice(t * P, (t + 1) * P))
                v.tensor_tensor(hT_lo[cut], bank[6 + t][:, :].rearrange("p (k q) -> p k q", k=4),
                                hT_hi[cut].bitcast(F32), ALU.subtract).then_inc(yT_ready, 1)

        for n in range(2 * DB):
            at = (*front(C_O + n), U_IN_END + 8 * n)
            split_steps(*at, 0, 4)
            if n == 0:
                dve.wait_ge(ot_evac, 17)
                dve.wait_ge(split_used, U_IN_END + CREDIT)
                o_split(qk[:, 16:20, :], hT_hi[:, 8:12, :], hT_lo[:, 8:12, :])
                split_steps(*at, 4, 6)
                o_split(qk[:, 20:24, :], hT_hi[:, 12:16, :], hT_lo[:, 12:16, :]).then_inc(oT_split, 1)
                split_steps(*at, 6, 8)
                later_vectors()
                continue
            gate_out(n - 1)
            if n in (4, 6):
                y_low(n // 2 - 2)
            split_steps(*at, 4, 8)

        def router_weights():
            dve.wait_ge(router_loaded, 64)
            col = lambda n: vecs[:, n, :].unsqueeze(2).broadcast_to([P, KB, 36])
            v.tensor_tensor(swr[:, :, :], wr[:, :, :], col(1), ALU.mult)
            dve.drain()
            v.tensor_reduce(swp[:, :], swr[:, :, :].rearrange("p k n -> p n k"), AX.X, ALU.add).then_inc(shift_in, 1)
            v.tensor_tensor(wr[:, :, :], wr[:, :, :], col(2), ALU.mult)
            v.tensor_tensor(fold[:, :], ident[:, 0:36], ident[:, 64:100], ALU.add)

        def y_out(nb):
            for t in range(TT):
                dve.wait_ge(y2_squared, 2 * nb + t + 1)
                if nb == DB - 1 and t == TT - 1:
                    v.tensor_reduce(ssq[:, 1, :], ssq_part[:, :, :], AX.X, ALU.add)
                    dve.drain()
                    v.tensor_scalar(inv[:, 1, :], ssq[:, 1, :], 1.0 / D, EPS, ALU.mult, ALU.add)
                    dve.drain()
                    v.reciprocal(inv[:, 1, :], inv[:, 1, :]).then_inc(inv_ready, 1)
                cut = slice(nb * NB, (nb + 1) * NB)
                last = v.tensor_tensor(y2[:, t, cut], bank[Y_BANKS[nb % 2][t]][:, :], rowGm[:, cut], ALU.mult)
            last.then_inc(y2_evac, 1)

        for n in range(8, 16):
            split_steps(*front(C_O + n), U_IN_END + 8 * n, 0, 4, wo_hi, wo_lo)
            if n == 8:
                gate_out(2 * DB - 1)
                split_steps(*front(C_O + n), U_IN_END + 8 * n, 4, 6, wo_hi, wo_lo)
                y_low(2)
            elif n == 9:
                y_low(3)
            elif n == 11:
                dve.wait_ge(rowm_loaded, 16)
            if n % 2 == 1 and n > 10:
                y_out((n - 11) // 2)
            if n == 12:
                dve.wait_ge(rconst_ready, 1)
                router_weights()
            if n == 14:
                dve.wait_ge(shift_done, 1)
                v.tensor_tensor(rbias[:, :], rbias[:, :], bank[6][:, 0:36], ALU.add).then_inc(shift_in, 1)
            split_steps(*front(C_O + n), U_IN_END + 8 * n, 6 if n == 8 else 4, 8, wo_hi, wo_lo)
        y_out(DB - 1)

        dve.wait_ge(x_again, 16)
        dve.wait_ge(rstd_ready, 2)
        dve.drain()
        for t in range(TT):
            for nb in range(DB):
                cut = slice(nb * NB, (nb + 1) * NB)
                v.scalar_tensor_tensor(xres[:, t, cut], y2[:, t, cut], rstd[:, 1, t:t + 1], xres[:, t, cut],
                                       ALU.mult, ALU.add).then_inc(x2_ready, 1)
        for g in range(DB):
            dve.wait_ge(x2T_done, DB + g + 1)
            v.tensor_copy(x2T[:, 4 * g:4 * g + 4, P:T], bank[DB + g][:, :].rearrange("p (k q) -> p k q", k=4))\
                .then_inc(x2T_evac1, 1)
        for t in range(TT):
            dve.wait_ge(logT_done, t + 1)
            for at in (0, 64):
                v.tensor_copy(logT[at:at + 36, t * P:(t + 1) * P], bank[t][at:at + 36, 0:P]).then_inc(logT_evac, 1)
        inverse(2, 2)

        def wide(ap, n):
            return ap.unsqueeze(2).broadcast_to([P, TT, n])

        def ranked(tmp, vals, top, n):
            for t in range(TT):
                v.scalar_tensor_tensor(tmp[:, t, :], vals[:, t, :], top[:, t:t + 1], desc[:, 0:n], ALU.is_equal,
                                       ALU.mult)
            dve.drain()
            v.tensor_reduce(m3[:, 3, :], tmp, AX.X, ALU.max)
            dve.drain()

        dve.wait_ge(rconst_ready, 1)
        dve.wait_ge(logits_done, TT)
        for t in range(TT):
            v.scalar_tensor_tensor(lg[:, t, :], bank[2][:, t * 64:t * 64 + 36], rstd[:, 2, t:t + 1], rbias[:, :], ALU.mult,
                                   ALU.add)
        dve.drain()
        v.tensor_reduce(m3[:, 0, :], lg[:, :, 0:GROUPS], AX.X, ALU.max)
        dve.drain()
        ranked(tg[:, :, :], lg[:, :, 0:GROUPS], m3[:, 0, :], GROUPS)
        for t in range(TT):
            v.tensor_scalar(tg[:, t, :], tg[:, t, :], m3[:, 3, t:t + 1], 1e30, ALU.subtract, ALU.mult)
        dve.drain()
        for t in range(TT):
            v.tensor_tensor(em[:, t, :].rearrange("p (g e) -> p g e", g=GROUPS),
                            lg[:, t, GROUPS:36].rearrange("p (g e) -> p g e", g=GROUPS),
                            tg[:, t, :].unsqueeze(2).broadcast_to([P, GROUPS, PER_GROUP]), ALU.add)
        dve.drain()
        v.tensor_reduce(m3[:, 1, :], em[:, :, :], AX.X, ALU.max)
        dve.drain()
        ranked(te[:, :, :], em[:, :, :], m3[:, 1, :], E)
        v.tensor_tensor(oh1[:, :, :], te[:, :, :], wide(m3[:, 3, :], E), ALU.is_equal)
        dve.drain()
        v.scalar_tensor_tensor(em[:, :, :], oh1[:, :, :], -1e32, em[:, :, :], ALU.mult, ALU.add)
        dve.drain()
        v.tensor_reduce(m3[:, 2, :], em[:, :, :], AX.X, ALU.max)
        dve.drain()
        ranked(te[:, :, :], em[:, :, :], m3[:, 2, :], E)
        for t in range(TT):
            v.scalar_tensor_tensor(em[:, t, :], te[:, t, :], m3[:, 3, t:t + 1], oh1[:, t, :], ALU.is_equal, ALU.add)
        dve.drain().then_inc(hot_ready, 1)
        v.tensor_tensor(oh2[:, :, :], te[:, :, :], wide(m3[:, 3, :], E), ALU.is_equal)
        v.tensor_tensor(ex[:, :, 0:GROUPS], lg[:, :, 0:GROUPS], wide(m3[:, 0, :], GROUPS), ALU.subtract)
        v.tensor_tensor(ex[:, :, 4], m3[:, 2, :], m3[:, 1, :], ALU.subtract)
        dve.drain().then_inc(ex_in, 1)
        dve.wait_ge(rank_done, 1)
        v.tensor_tensor(rank[:, :, 0:E], bank[5][:, 0:2 * E].rearrange("p (t e) -> p t e", t=TT), em[:, :, :],
                        ALU.mult)
        dve.drain()

        def pick_pair(r1, first=False):
            if not first:
                dve.wait_ge(got_done, r1 * 4)
            for t in range(TT):
                last = v.tensor_tensor(pick[:, t, :, :],
                                       iota[:, 1:CAP + 1].unsqueeze(1).broadcast_to([P, 2, CAP]),
                                       rank[:, t, bass.ds(r1 * 2, 2)].unsqueeze(2).broadcast_to([P, 2, CAP]),
                                       ALU.is_equal)
            last.then_inc(picked, 1)

        pick_pair(0, first=True)
        dve.wait_ge(ex_done, 1)
        v.tensor_reduce(m3[:, 0, :], ex[:, :, 0:GROUPS], AX.X, ALU.add)
        dve.drain()
        v.scalar_tensor_tensor(m3[:, 0, :], ex[:, :, 4], 1.0, m3[:, 0, :], ALU.add, ALU.mult)
        dve.drain()
        v.reciprocal(m3[:, 1, :], m3[:, 0, :])
        dve.drain()
        v.tensor_tensor(m3[:, 2, :], m3[:, 1, :], ex[:, :, 4], ALU.mult)
        v.tensor_tensor(oh1[:, :, :], oh1[:, :, :], wide(m3[:, 1, :], E), ALU.mult)
        dve.drain()
        v.tensor_tensor(oh2[:, :, :], oh2[:, :, :], wide(m3[:, 2, :], E), ALU.mult)
        dve.drain()
        v.tensor_tensor(wtok[:, :, 0:E], oh1[:, :, :], oh2[:, :, :], ALU.add)
        dve.drain().then_inc(tables_ready, 1)
        dve.wait_ge(count_done, 1)
        v.tensor_scalar(cnt[:, :], bank[2][:, 2 * E:3 * E], float(CAP), None, ALU.is_gt)
        for n in (2, 3):
            v.tensor_scalar(te[:, n - 2, :], bank[2][:, 2 * E:3 * E], float(CAP * n), None, ALU.is_gt)
        dve.drain()
        for n in (0, 1):
            v.tensor_tensor(cnt[:, :], cnt[:, :], te[:, n, :], ALU.add)
            dve.drain()
        v.tensor_tensor_scan(cum[:, :], ones[:, 0:E], cnt[:, :], 0.0, ALU.mult, ALU.add)
        dve.drain()
        v.tensor_tensor(cmpj[:, :, :], cum[:, :].unsqueeze(1).broadcast_to([P, 8, E]),
                        iota[:, 0:8].unsqueeze(2).broadcast_to([P, 8, E]), ALU.is_le)
        v.tensor_tensor(cnt[:, :], cum[:, :], cnt[:, :], ALU.subtract)
        v.tensor_scalar(te[:, :, :], rank[:, :, 0:E], CAP + 0.5, None, ALU.is_gt)
        v.tensor_copy(whole[:, 8:9], cum[:, E - 1:E])
        dve.drain()
        v.tensor_reduce(eidf[:, :], cmpj[:, :, :], AX.X, ALU.add)
        v.tensor_scalar(cnt[:, :], cnt[:, :], float(CAP), -float(CAP), ALU.mult, ALU.add)
        dve.drain()
        v.tensor_scalar(whole[:, 0:8], eidf[:, :], float(E - 1), None, ALU.min)
        v.tensor_tensor(over[:, :, :], rank[:, :, 0:E], cnt[:, :].unsqueeze(1).broadcast_to([P, TT, E]), ALU.add)
        dve.drain()
        v.tensor_tensor(over[:, :, :], over[:, :, :], te[:, :, :], ALU.mult)
        dve.drain()
        v.tensor_scalar(over[:, :, :], over[:, :, :], -1.0, None, ALU.add)
        dve.drain().then_inc(tables_ready, 1)

        def send_matrix(rows, weight_col):
            return v.tensor_scalar(send[0:rows, :], iota[0:rows, :], slot[0:rows, weight_col[0]:weight_col[0] + 1],
                                   weight_col[1], ALU.is_equal, ALU.mult)

        def gate_rows(nb):
            for t in range(TT):
                cut = slice(nb * NB, (nb + 1) * NB)
                v.tensor_tensor(acc_g[:, t, cut], acc[:, t, cut], rowGf[:, cut], ALU.mult)

        def pair(r, last=False):
            dve.wait_ge(slots_evac, r + 1)
            for e in range(2):
                v.tensor_copy(wsel[CAP * e:CAP * e + CAP, 0:1], slot[CAP * e:CAP * e + CAP, bass.ds(r * 2 + e, 1)])
                v.tensor_copy(wsel[CAP * e:CAP * e + CAP, 1:2], slot[CAP * e:CAP * e + CAP, 34:35])
            dve.drain()
            if not last:
                pick_pair(r + 1)
            dve.wait_ge(comb_done, r * 8 + 8)
            v.tensor_scalar(send[:, :], iota[:, :], wsel[:, 1:2], wsel[:, 0:1], ALU.is_equal, ALU.mult)\
                .then_inc(send_ready, 1)
            for e in range(2):
                dve.wait_ge(sig_done, r * 2 + (e + 1))
                v.tensor_tensor(act[:, e, :], act[:, e, :], bank[e][:, 0:T], ALU.mult)
                dve.drain()
                v.tensor_tensor(act[:, e, :], act[:, e, :], bank[e][:, T:2 * T], ALU.mult).then_inc(act_ready, 1)
            for nb in range(DB):
                for t in range(TT):
                    dve.wait_ge(comb_done, r * 8 + (nb * 2 + t + 9))
                    cut = acc[:, t, nb * NB:(nb + 1) * NB]
                    v.tensor_tensor(cut, cut, bank[5 + t][:, :], ALU.add).then_inc(comb_added, 1)
                if last and nb in (1, 2):
                    if nb == 1:
                        dve.wait_ge(rowf_loaded, 16)
                    gate_rows(nb - 1)

        dve.wait_ge(acc_zero, 1)
        with dve.Fori(0, E // 4 - 1) as i:
            for x2 in range(2):
                pair(i * 2 + x2)
        pair(LAST - 1)
        pair(LAST, last=True)
        dve.drain()
        gate_rows(2)

        dve.wait_ge(comb_added, 4 * E + 2)
        dve.sem_inc(ov_go, 1)
        n_over = dve.value_load(whole[0:1, 8:9], min_val=0, max_val=MAX_OVER)
        with dve.If(n_over > 0):
            dve.wait_ge(got_done, 2 * E)
            with dve.Fori(0, n_over) as j:
                v.tensor_scalar(te[:, :, :], over[:, :, :], -0.5, None, ALU.is_gt)
                v.tensor_scalar(oh1[:, :, :], over[:, :, :], CAP - 0.5, None, ALU.is_lt)
                dve.drain()
                v.tensor_tensor(te[:, :, :], te[:, :, :], oh1[:, :, :], ALU.mult)
                dve.drain()
                v.scalar_tensor_tensor(oh1[:, :, :], over[:, :, :], 1.0, te[:, :, :], ALU.add, ALU.mult)
                v.tensor_tensor(oh2[:, :, :], wtok[:, :, 0:E], te[:, :, :], ALU.mult)
                dve.drain()
                v.tensor_reduce(rover[:, :], oh1[:, :, :], AX.X, ALU.add)
                v.tensor_reduce(tover[:, :, 0], oh2[:, :, :], AX.X, ALU.add)
                v.tensor_copy(tover[:, :, 1], wtok[:, :, 34])
                v.tensor_scalar(over[:, :, :], over[:, :, :], -float(CAP), None, ALU.add)
                dve.drain()
                v.tensor_scalar(rover[:, :], rover[:, :], -1.0, None, ALU.add)
                dve.drain()
                for t in range(TT):
                    last = v.tensor_scalar(pick[:, t, 0, :], iota[:, 0:CAP], rover[:, t:t + 1], None, ALU.is_equal)
                last.then_inc(ov_pick, 1)
                dve.wait_ge(ov_in, j + 1)
                v.tensor_scalar(send[0:CAP, :], iota[0:CAP, :], slot[0:CAP, 1:2], slot[0:CAP, 0:1],
                                ALU.is_equal, ALU.mult)
                dve.wait_ge(ov_sig, j + 1)
                v.tensor_tensor(act[:, 0, :], act[:, 0, :], bank[0][:, 0:T], ALU.mult)
                dve.drain()
                v.tensor_tensor(act[:, 0, :], act[:, 0, :], bank[0][:, T:2 * T], ALU.mult).then_inc(ov_act, 1)
                dve.wait_ge(ov_comb, j + 1)
                for nb in range(DB):
                    for t in range(TT):
                        cut = acc[:, t, nb * NB:(nb + 1) * NB]
                        last = v.tensor_tensor(cut, cut, bank[2 * nb + t][:, :], ALU.add)
                last.then_inc(ov_go, 1)
            dve.drain().then_inc(ov_done, 1)
            for nb in range(DB - 1):
                gate_rows(nb)
        dve.wait_ge(ssq_done, 3)
        v.tensor_reduce(ssq[:, 3, :], ssq_part[:, :, :], AX.X, ALU.add)
        dve.drain()
        v.tensor_scalar(inv[:, 3, :], ssq[:, 3, :], 1.0 / D, EPS, ALU.mult, ALU.add)
        dve.drain()
        v.reciprocal(inv[:, 3, :], inv[:, 3, :]).then_inc(inv_ready, 1)
        gate_rows(3)
        dve.wait_ge(rstd_ready, 4)
        dve.drain()
        for t in range(TT):
            for nb in range(DB):
                cut = slice(nb * NB, (nb + 1) * NB)
                v.scalar_tensor_tensor(xres[:, t, cut], acc_g[:, t, cut], rstd[:, 3, t:t + 1], xres[:, t, cut],
                                       ALU.mult, ALU.add).then_inc(fin_ready, 1)

    block.__exit__(None, None, None)


_INS = ["x", "c", "w_ada", "b_ada", "g_pre_mix", "g_post_mix", "w_in", "swa_sinks", "w_o_moba", "w_o_swa", "w_out",
        "g_pre_ffn", "g_post_ffn", "w_router_group", "b_router_group", "w_router_expert", "b_router_expert",
        "w_gate", "w_up", "w_down"]


def kernel(**inputs):
    import numpy as np
    import concourse.bacc as bacc
    from concourse import mybir as _mybir
    from concourse.bass_utils import run_bass_kernel_spmd

    nc = bacc.Bacc("TRN2", target_bir_lowering=False, num_devices=1)
    arrays, args = {}, []
    for name in _INS:
        a = np.ascontiguousarray(inputs[name])
        arrays[f"in_{name}"] = a
        args.append(nc.dram_tensor(f"in_{name}", a.shape, _mybir.dt.from_np(a.dtype), kind="ExternalInput").ap())
    out = nc.dram_tensor("out_0", (1, T, D), F32, kind="ExternalOutput").ap()
    decoder_block(nc, *args, out)
    r = run_bass_kernel_spmd(nc, [arrays], core_ids=[0])
    return r.results[0]["out_0"]
```
